# Optimizing a Trainium2 kernel written in Bass

```python
import math
import jax
import jax.numpy as jnp
from jax import lax
import numpy as np

D_MODEL = 1024
BATCH = 1
SEQ = 256
DEPTH = 1

N_ATTN_HEADS = 8
HEAD_DIM = 64
D_ATTN = N_ATTN_HEADS * HEAD_DIM
ROT_DIM = HEAD_DIM // 4
ROPE_THETA = 500000.0
MOBA_BLOCK = 256
MOBA_TOPK = 3
MOBA_Q_CHUNK = 32

N_SSM_HEADS = 16
SSM_HEAD_DIM = 64
D_SSM = N_SSM_HEADS * SSM_HEAD_DIM
SSM_GROUPS = 2
SSM_HEADS_PER_GROUP = N_SSM_HEADS // SSM_GROUPS
D_STATE = 128
CONV_K = 4
SSD_CHUNK = 256
D_CONV = D_SSM + 2 * SSM_GROUPS * D_STATE
DT_MIN = 0.001
DT_MAX = 0.1

D_MIX = D_ATTN + D_SSM
D_IN_PROJ = 3 * D_ATTN + D_SSM + D_CONV + N_SSM_HEADS
SPLIT_POINTS = (D_ATTN, 2 * D_ATTN, 3 * D_ATTN, 3 * D_ATTN + D_SSM, 3 * D_ATTN + D_SSM + D_CONV)
D_FF = 2816
FFN_RESIDUAL_WEIGHT = 0.5
EPS = 1e-6

kernel_name = "hymba_moba_ssd_macaron_layer"

def rms_norm(x, w):
    xf = x.astype(jnp.float32)
    y = xf * lax.rsqrt(jnp.mean(xf * xf, axis=-1, keepdims=True) + EPS)
    return (y * w.astype(jnp.float32)).astype(x.dtype)

def swiglu(h, w1, w3, w2):
    return (jax.nn.silu(h @ w1) * (h @ w3)) @ w2

def pad_seq(t, axis, multiple):
    pad = (-t.shape[axis]) % multiple
    widths = [(0, 0)] * t.ndim
    widths[axis] = (0, pad)
    return jnp.pad(t, widths)

def rotary_tables(seq_len):
    inv_freq = ROPE_THETA ** (-jnp.arange(0, ROT_DIM, 2, dtype=jnp.float32) / ROT_DIM)
    ang = jnp.arange(seq_len, dtype=jnp.float32)[:, None] * inv_freq[None, :]
    return jnp.cos(ang), jnp.sin(ang)

def partial_rotary(t, cos, sin):
    half = ROT_DIM // 2
    tf = t[..., :ROT_DIM].astype(jnp.float32)
    r1, r2 = tf[..., :half], tf[..., half:]
    rot = jnp.concatenate([r1 * cos - r2 * sin, r2 * cos + r1 * sin], axis=-1)
    return jnp.concatenate([rot.astype(t.dtype), t[..., ROT_DIM:]], axis=-1)

def moba_attention(q, k, v):
    Bn, Hn, S, Dh = q.shape
    q, k, v = (pad_seq(t, 2, MOBA_BLOCK) for t in (q, k, v))
    S_pad = q.shape[2]
    nb = S_pad // MOBA_BLOCK
    topk = min(MOBA_TOPK, nb)
    kb = k.reshape(Bn, Hn, nb, MOBA_BLOCK, Dh)
    vb = v.reshape(Bn, Hn, nb, MOBA_BLOCK, Dh)
    k_mean = jnp.mean(kb.astype(jnp.float32), axis=3)
    n_chunks = S_pad // MOBA_Q_CHUNK
    q_chunks = jnp.moveaxis(q.reshape(Bn, Hn, n_chunks, MOBA_Q_CHUNK, Dh), 2, 0)
    b_idx = jnp.arange(Bn)[:, None, None, None]
    h_idx = jnp.arange(Hn)[None, :, None, None]
    scale = Dh ** -0.5
    L = MOBA_BLOCK

    def one_chunk(args):
        q_c, c = args
        q_pos = c * MOBA_Q_CHUNK + jnp.arange(MOBA_Q_CHUNK)
        own = (c * MOBA_Q_CHUNK) // MOBA_BLOCK
        gate = jnp.einsum('bhqd,bhnd->bhqn', q_c.astype(jnp.float32), k_mean)
        fully_past = jnp.arange(nb) < own
        gate = jnp.where(fully_past, gate, -jnp.inf)
        top_val, top_idx = lax.top_k(gate, topk)
        valid = jnp.isfinite(top_val)
        k_sel = kb[b_idx, h_idx, top_idx]
        v_sel = vb[b_idx, h_idx, top_idx]
        s_sel = jnp.einsum('bhqd,bhqjld->bhqjl', q_c, k_sel).astype(jnp.float32) * scale
        s_sel = jnp.where(valid[..., None], s_sel, -jnp.inf).reshape(Bn, Hn, MOBA_Q_CHUNK, topk * L)
        k_own = lax.dynamic_index_in_dim(kb, own, axis=2, keepdims=False)
        v_own = lax.dynamic_index_in_dim(vb, own, axis=2, keepdims=False)
        s_own = jnp.einsum('bhqd,bhld->bhql', q_c, k_own).astype(jnp.float32) * scale
        k_pos = own * MOBA_BLOCK + jnp.arange(MOBA_BLOCK)
        s_own = jnp.where(k_pos[None, :] <= q_pos[:, None], s_own, -jnp.inf)
        p = jax.nn.softmax(jnp.concatenate([s_sel, s_own], axis=-1), axis=-1).astype(v.dtype)
        p_sel = p[..., :topk * L].reshape(Bn, Hn, MOBA_Q_CHUNK, topk, L)
        p_own = p[..., topk * L:]
        return (jnp.einsum('bhqjl,bhqjld->bhqd', p_sel, v_sel)
                + jnp.einsum('bhql,bhld->bhqd', p_own, v_own))

    out = lax.map(one_chunk, (q_chunks, jnp.arange(n_chunks)))
    out = jnp.moveaxis(out, 0, 2).reshape(Bn, Hn, S_pad, Dh)
    return out[:, :, :S]

def causal_depthwise_conv(u, w, b):
    C = u.shape[-1]
    y = lax.conv_general_dilated(u, w[:, None, :].astype(u.dtype), window_strides=(1,),
                                 padding=[(CONV_K - 1, 0)],
                                 dimension_numbers=('NWC', 'WIO', 'NWC'),
                                 feature_group_count=C)
    return y + b

def segsum(a):
    T = a.shape[-1]
    cs = jnp.cumsum(a, axis=-1)
    diff = cs[..., :, None] - cs[..., None, :]
    mask = jnp.tril(jnp.ones((T, T), dtype=bool))
    return jnp.where(mask, diff, -jnp.inf)

def ssd_mixer(z, xBC, dt_raw, conv_w, conv_b, dt_bias, A_log, D_skip, norm_w):
    Bn, S, _ = xBC.shape
    G, R, P, N, Lc = SSM_GROUPS, SSM_HEADS_PER_GROUP, SSM_HEAD_DIM, D_STATE, SSD_CHUNK
    xBC = jax.nn.silu(causal_depthwise_conv(xBC, conv_w, conv_b))
    xs, Bm, Cm = jnp.split(xBC, (D_SSM, D_SSM + G * N), axis=-1)
    dt = jax.nn.softplus(dt_raw.astype(jnp.float32) + dt_bias.astype(jnp.float32))
    A = -jnp.exp(A_log.astype(jnp.float32)).reshape(G, R)
    xs, Bm, Cm, dt = (pad_seq(t, 1, Lc) for t in (xs, Bm, Cm, dt))
    S_pad = xs.shape[1]
    nc = S_pad // Lc
    X = xs.reshape(Bn, nc, Lc, G, R, P)
    Bc = Bm.reshape(Bn, nc, Lc, G, N)
    Cc = Cm.reshape(Bn, nc, Lc, G, N)
    dtc = dt.reshape(Bn, nc, Lc, G, R)
    a = jnp.transpose(dtc * A, (0, 3, 4, 1, 2))
    a_cs = jnp.cumsum(a, axis=-1)
    Xdt = X * dtc[..., None]
    decay_in = jnp.exp(segsum(a))
    CB = jnp.einsum('bclgn,bcsgn->bgcls', Cc, Bc)
    y_diag = jnp.einsum('bgrcls,bcsgrp->bclgrp', CB[:, :, None] * decay_in, Xdt)
    decay_states = jnp.exp(a_cs[..., -1:] - a_cs)
    states = jnp.einsum('bclgn,bgrcl,bclgrp->bcgrpn', Bc, decay_states, Xdt)
    states = jnp.concatenate([jnp.zeros_like(states[:, :1]), states], axis=1)
    a_last = jnp.pad(a_cs[..., -1], ((0, 0), (0, 0), (0, 0), (1, 0)))
    decay_chunk = jnp.exp(segsum(a_last))
    states = jnp.einsum('bgrzc,bcgrpn->bzgrpn', decay_chunk, states)[:, :-1]
    y_off = jnp.einsum('bclgn,bcgrpn,bgrcl->bclgrp', Cc, states, jnp.exp(a_cs))
    y = y_diag + y_off + X * D_skip.astype(jnp.float32).reshape(G, R)[:, :, None]
    y = y.reshape(Bn, S_pad, D_SSM)[:, :S]
    y = y * jax.nn.silu(z.astype(jnp.float32))
    y = rms_norm(y.reshape(Bn, S, G, D_SSM // G), norm_w.reshape(G, D_SSM // G))
    return y.reshape(Bn, S, D_SSM).astype(z.dtype)

def setup_inputs(seed: int = 0) -> dict:
    key = jax.random.key(seed)
    ks = jax.random.split(key, 20)
    f32 = jnp.float32

    def normal(k, shape, scale):
        return jax.random.normal(k, shape, f32) * scale

    def gain(k, shape):
        return 1.0 + 0.02 * jax.random.normal(k, shape, f32)

    dt_init = jnp.exp(jax.random.uniform(ks[9], (DEPTH, N_SSM_HEADS), f32,
                                         math.log(DT_MIN), math.log(DT_MAX)))
    return {
        "x": normal(ks[0], (BATCH, SEQ, D_MODEL), 1.0),
        "ffn1_norm": gain(ks[1], (DEPTH, D_MODEL)),
        "ffn1_w1": normal(ks[2], (DEPTH, D_MODEL, D_FF), D_MODEL ** -0.5),
        "ffn1_w3": normal(ks[3], (DEPTH, D_MODEL, D_FF), D_MODEL ** -0.5),
        "ffn1_w2": normal(ks[4], (DEPTH, D_FF, D_MODEL), D_FF ** -0.5),
        "mix_norm": gain(ks[5], (DEPTH, D_MODEL)),
        "w_in": normal(ks[6], (DEPTH, D_MODEL, D_IN_PROJ), D_MODEL ** -0.5),
        "conv_w": normal(ks[7], (DEPTH, CONV_K, D_CONV), CONV_K ** -0.5),
        "conv_b": normal(ks[8], (DEPTH, D_CONV), 0.01),
        "dt_bias": dt_init + jnp.log(-jnp.expm1(-dt_init)),
        "A_log": jnp.log(jax.random.uniform(ks[10], (DEPTH, N_SSM_HEADS), f32, 1.0, 16.0)),
        "D_skip": 1.0 + 0.1 * jax.random.normal(ks[11], (DEPTH, N_SSM_HEADS), f32),
        "attn_out_norm": gain(ks[12], (DEPTH, D_ATTN)),
        "ssd_out_norm": gain(ks[13], (DEPTH, D_SSM)),
        "w_out": normal(ks[14], (DEPTH, D_MIX, D_MODEL), D_MIX ** -0.5),
        "ffn2_norm": gain(ks[15], (DEPTH, D_MODEL)),
        "ffn2_w1": normal(ks[16], (DEPTH, D_MODEL, D_FF), D_MODEL ** -0.5),
        "ffn2_w3": normal(ks[17], (DEPTH, D_MODEL, D_FF), D_MODEL ** -0.5),
        "ffn2_w2": normal(ks[18], (DEPTH, D_FF, D_MODEL), D_FF ** -0.5),
        "final_norm": gain(ks[19], (D_MODEL,)),
    }

def reference(x, ffn1_norm, ffn1_w1, ffn1_w3, ffn1_w2, mix_norm, w_in, conv_w, conv_b,
              dt_bias, A_log, D_skip, attn_out_norm, ssd_out_norm, w_out,
              ffn2_norm, ffn2_w1, ffn2_w3, ffn2_w2, final_norm):
    Bn, S, _ = x.shape
    cos, sin = rotary_tables(S)

    def heads(t):
        return t.reshape(Bn, S, N_ATTN_HEADS, HEAD_DIM).transpose(0, 2, 1, 3)

    for l in range(DEPTH):
        h = rms_norm(x, ffn1_norm[l])
        x = x + FFN_RESIDUAL_WEIGHT * swiglu(h, ffn1_w1[l], ffn1_w3[l], ffn1_w2[l])
        h = rms_norm(x, mix_norm[l])
        proj = h @ w_in[l]
        q, k, v, z, xBC, dt_raw = jnp.split(proj, SPLIT_POINTS, axis=-1)
        attn = moba_attention(partial_rotary(heads(q), cos, sin),
                              partial_rotary(heads(k), cos, sin), heads(v))
        attn = rms_norm(attn.transpose(0, 2, 1, 3).reshape(Bn, S, D_ATTN), attn_out_norm[l])
        ssd = ssd_mixer(z, xBC, dt_raw, conv_w[l], conv_b[l], dt_bias[l], A_log[l],
                        D_skip[l], ssd_out_norm[l])
        x = x + jnp.concatenate([attn, ssd], axis=-1) @ w_out[l]
        h = rms_norm(x, ffn2_norm[l])
        x = x + FFN_RESIDUAL_WEIGHT * swiglu(h, ffn2_w1[l], ffn2_w3[l], ffn2_w2[l])
    return rms_norm(x, final_norm)


_drawn_inputs = setup_inputs


def setup_inputs(seed=0):
    import zlib

    import numpy as np

    out = dict(_drawn_inputs(seed))
    spreads = {}
    factors = {'ffn1_norm': 4.797,
     'conv_b': 7.336,
     'attn_out_norm': 6.924,
     'ssd_out_norm': 4.88,
     'ffn2_norm': 8.0,
     'final_norm': 2.846}
    for name, (base, spread) in spreads.items():
        noise = np.random.default_rng([zlib.crc32(name.encode()), seed]).standard_normal(out[name].shape)
        drawn = base * np.exp(spread * noise) if base else spread * noise
        out[name] = jnp.asarray(drawn.astype(out[name].dtype))
    for name, factor in factors.items():
        out[name] = (out[name] * factor).astype(out[name].dtype)
    return out
```

```python
from contextlib import ExitStack

import numpy as np
import concourse.bass as bass
from concourse import mybir

P = 128
SEQ, D, F = 256, 1024, 2816
TT = SEQ // P
KD = D // P
HEADS, HD, ROT = 8, 64, 16
D_ATTN = HEADS * HD
SH, SP_, GROUPS = 16, 64, 2
D_SSM = SH * SP_
N_STATE, TAPS = 128, 4
D_CONV = D_SSM + 2 * GROUPS * N_STATE
D_IN = 3 * D_ATTN + D_SSM + D_CONV + SH
D_MIX = D_ATTN + D_SSM
CT = D_CONV // P
EPS = 1e-6
THETA = 500000.0
MASKED = -(2.0 ** 99)

RAW_SLOTS, HALF_SLOTS = 3, 6
HALF = 1024
FT = F // P
FI = FT // 2

MIX_UNIT0 = 3 * FI
CONV_ORDER = (8, 9, 10, 11, 0, 1, 2, 3, 4, 5, 6, 7)
CHUNKS = ("z0", "z1", "q", "k", "v")
CHUNK_COL = {"q": 0, "k": D_ATTN, "v": 2 * D_ATTN, "z0": 3 * D_ATTN, "z1": 3 * D_ATTN + 512}
OUT_ROWS = (4, 5, 6, 7, 8, 9, 10, 11, 0, 1, 2, 3)
MIX_HALVES = 12 + 4 * len(CHUNKS) + 12
MIX_UNITS = MIX_HALVES // 2
MIX_HALF0 = 6 * FI
FFN_UNIT0 = (0, MIX_UNIT0 + MIX_UNITS)
FFN_HALF0 = (0, MIX_HALF0 + MIX_HALVES)
M_CHUNK = {c: 12 + 4 * j for j, c in enumerate(CHUNKS)}
M_OUT = 12 + 4 * len(CHUNKS)

C_ID, C_TRI, C_MASK, C_COS, C_SIN, C_END = 0, 128, 384, 512, 544, 576

def mix_row(r):
    return {0: 4, 1: 8, 2: 0}[r // 4] + r % 4


def shape_constants():
    c = np.zeros((P, C_END), np.float32)
    c[:, C_ID:C_ID + P] = np.eye(P)
    c[:, C_TRI:C_TRI + P] = np.triu(np.ones((P, P)))
    c[:, C_TRI + P:C_TRI + 2 * P] = 1.0
    c[:, C_MASK:C_MASK + P] = np.where(np.triu(np.ones((P, P))) > 0, 0.0, MASKED)
    inv = (np.float32(THETA) ** (-np.arange(0, ROT, 2, dtype=np.float32) / np.float32(ROT))).astype(np.float32)
    ang = np.arange(SEQ, dtype=np.float32)[:, None] * inv[None, :]
    cos, sin = (f(ang).astype(np.float32).reshape(TT, P, ROT // 2).transpose(1, 0, 2) for f in (np.cos, np.sin))
    c[:, C_COS:C_COS + TT * ROT] = np.concatenate([cos, cos], -1).reshape(P, -1)
    c[:, C_SIN:C_SIN + TT * ROT] = np.concatenate([-sin, sin], -1).reshape(P, -1)
    return c


def build(nc, x_in, w1s, w3s, w2s, norms, w_in, conv_w, conv_b, dt_bias, A_log, D_skip,
          attn_norm, ssd_norm, w_out, consts, out):
    f32, f32r = mybir.dt.float32, mybir.dt.float32r
    ALU, ACT, AX = mybir.AluOpType, mybir.ActivationFunctionType, mybir.AxisListType

    with ExitStack() as ctx:
        def sb(name, shape, dtype=f32):
            return ctx.enter_context(nc.sbuf_tensor(name, shape, dtype))

        def sem(name):
            return ctx.enter_context(nc.semaphore(name))

        raw = sb("raw", [P, RAW_SLOTS, 2 * HALF])
        w_hi = sb("w_hi", [P, HALF_SLOTS, HALF], f32r)
        w_lo = sb("w_lo", [P, HALF_SLOTS, HALF], f32r)
        x = sb("x", [P, TT, D])
        hT_hi = sb("hT_hi", [P, 12, SEQ], f32r)
        hT_lo = sb("hT_lo", [P, 12, SEQ], f32r)
        normed = sb("normed", [P, TT, D_MIX])
        norm_w = sb("norm_w", [P, 2, D])
        mix_w = sb("mix_w", [P, D_MIX])
        cst = sb("cst", [P, C_END])
        ident_r = sb("ident_r", [P, P], f32r)
        mask_r = sb("mask_r", [P, P], f32r)
        small = sb("small", [P, 3, SH])
        conv_rows = sb("conv_rows", [(TAPS + 1) * CT, P])
        conv_p = sb("conv_p", [P, TAPS + 1, CT])
        wdt = sb("wdt", [P, KD, SH])
        wdt_hi = sb("wdt_hi", [P, KD, SH], f32r)
        wdt_lo = sb("wdt_lo", [P, KD, SH], f32r)
        sumsq = sb("sumsq", [P, 12])
        rstd = sb("rstd", [P, 12])
        minus_half = sb("minus_half", [P, 1])
        silu_g = sb("silu_g", [P, SEQ])
        gu = sb("gu", [P, SEQ])
        gu_hi = sb("gu_hi", [P, 2, SEQ], f32r)
        gu_lo = sb("gu_lo", [P, 2, SEQ], f32r)
        conv_acc = sb("conv_acc", [P, 2, SEQ])
        xbc = sb("xbc", [P, CT, SEQ])
        x_tok = sb("x_tok", [P, TT, D_SSM])
        z_silu = sb("z_silu", [P, TT, D_SSM])
        dts = sb("dts", [P, 8, TT, SH])
        csT_hi = sb("csT_hi", [SH, SEQ], f32r)
        csT_lo = sb("csT_lo", [SH, SEQ], f32r)
        cb = sb("cb", [P, GROUPS, 384])
        decay = sb("decay", [P, 2, 384])
        mix_m = sb("mix_m", [P, 2, 384])
        q_tok = sb("q_tok", [P, TT, D_ATTN])
        k_tok = sb("k_tok", [P, TT, D_ATTN])
        v_tok = sb("v_tok", [P, TT, D_ATTN])
        rot_t = sb("rot_t", [P, TT, HEADS, ROT])
        qT = sb("qT", [P, HEADS // 2, SEQ])
        kT = sb("kT", [P, HEADS // 2, SEQ])
        probs, probsT = decay, mix_m
        row_max = sb("row_max", [P, HEADS, TT])
        row_bias = sb("row_bias", [P, HEADS, TT])
        row_sum = sb("row_sum", [P, TT, HEADS])
        row_inv = sb("row_inv", [P, TT, HEADS])

        bank = ctx.enter_context(nc.psum_tensor("bank", [P, 8, 512], f32))
        G_BANK, U_BANK = 4, 5
        T_BANKS = ((6, 7), (4, 5))

        ident, tri = cst[:, C_ID:C_ID + P], cst[:, C_TRI:C_TRI + SEQ]
        cos_t = cst[:, C_COS:C_COS + TT * ROT].rearrange("p (t r) -> p t r", t=TT)
        sin_t = cst[:, C_SIN:C_SIN + TT * ROT].rearrange("p (t r) -> p t r", t=TT)
        skip16, bias16, alog16 = (small[:, j, :] for j in range(3))

        x_loaded = sem("x_loaded")
        consts_loaded = sem("consts_loaded")
        params_loaded = sem("params_loaded")
        norm_loaded = [sem(f"norm_loaded{n}") for n in range(4)]
        raw_loaded = [sem(f"raw_loaded{s}") for s in range(RAW_SLOTS)]
        hi_ready = sem("hi_ready")
        half_ready = sem("half_ready")
        half_used = sem("half_used")
        half_const = sem("half_const")
        consts_r = sem("consts_r")
        wdt_hi_ready = sem("wdt_hi_ready")
        wdt_ready = sem("wdt_ready")
        x_ready = sem("x_ready")
        sq_ready = sem("sq_ready")
        rstd_ready = sem("rstd_ready")
        pool_step = sem("pool_step")
        scaled = sem("scaled")
        transposed = sem("transposed")
        hT_hi_ready = sem("hT_hi_ready")
        hT_ready = sem("hT_ready")
        gate_done = sem("gate_done")
        up_done = sem("up_done")
        down_done = sem("down_done")
        silu_ready = sem("silu_ready")
        gu_ready = sem("gu_ready")
        gu_hi_ready = sem("gu_hi_ready")
        gu_split = sem("gu_split")
        acc_ready = sem("acc_ready")
        act_step = sem("act_step")
        dve_step = sem("dve_step")
        neg_a_ready = sem("neg_a_ready")
        conv_rows_T = sem("conv_rows_T")
        conv_p_ready = sem("conv_p_ready")
        dt_done = sem("dt_done")
        dt_arg = sem("dt_arg")
        dt_exp = sem("dt_exp")
        a_ready = sem("a_ready")
        cs_done = sem("cs_done")
        cs_tok_ready = sem("cs_tok_ready")
        csT_done = sem("csT_done")
        csT_ready = sem("csT_ready")
        tap_ready = sem("tap_ready")
        taps_done = sem("taps_done")
        xbc_ready = sem("xbc_ready")
        cb_done = sem("cb_done")
        cb_ready = sem("cb_ready")
        xT_done = sem("xT_done")
        x_tok_ready = sem("x_tok_ready")
        skip_ready = sem("skip_ready")
        proj_out = sem("proj_out")
        bc_done = sem("bc_done")
        decay_ready = sem("decay_ready")
        m_ready = sem("m_ready")
        y_done = sem("y_done")
        y_added = sem("y_added")
        gated = sem("gated")
        rotated = sem("rotated")
        qkT_done = sem("qkT_done")
        qkT_ready = sem("qkT_ready")
        scores_done = sem("scores_done")
        max_ready = sem("max_ready")
        probs_ready = sem("probs_ready")
        probsT_done = sem("probsT_done")
        probsT_ready = sem("probsT_ready")
        pv_done = sem("pv_done")
        final_ready = sem("final_ready")
        out_stored = sem("out_stored")

        block = ctx.enter_context(nc.Block())

        def cols_half(t, half):
            return t.rearrange("p (k f) -> p k f", k=KD)[:, :, half * P:(half + 1) * P]

        def by_tile(t):
            return t.rearrange("p (k f) -> p k f", k=KD)

        def ffn_half(n, i, odd, kind):
            h0 = FFN_HALF0[n] + 3 * odd + kind
            r = raw[:, (FFN_UNIT0[n] + kind) % RAW_SLOTS, :]
            src = cols_half(r, odd) if kind < 2 else r[:, odd * HALF:(odd + 1) * HALF]
            return h0 + 6 * i, h0 % HALF_SLOTS, src

        def mix_half(m):
            r = raw[:, (MIX_UNIT0 + m // 2) % RAW_SLOTS, :]
            src = cols_half(r, m % 2) if m < 12 else r[:, (m % 2) * HALF:(m % 2 + 1) * HALF]
            return MIX_HALF0 + m, (MIX_HALF0 + m) % HALF_SLOTS, src

        def ffn_load(eng, n, i, kind):
            s = (FFN_UNIT0[n] + kind) % RAW_SLOTS
            dst = raw[:, s, :]
            if kind < 2:
                src = (w1s, w3s)[kind][n].rearrange("(k p) f -> p k f", p=P)[:, :, bass.ts(i, 2 * P)]
                dst = dst.rearrange("p (k f) -> p k f", k=KD)
            else:
                src = w2s[n].rearrange("(t p) d -> p t d", p=P)[:, bass.ts(i, 2), :]
                dst = dst.rearrange("p (t d) -> p t d", t=2)
            eng.dma_start(dst, src).then_inc(raw_loaded[s], 16)

        def mix_load(eng, u):
            s = (MIX_UNIT0 + u) % RAW_SLOTS
            dst = raw[:, s, :]
            if u < 6:
                c = 3 * D_ATTN + D_SSM + CONV_ORDER[2 * u] * P
                src = w_in.rearrange("(k p) f -> p k f", p=P)[:, :, c:c + 2 * P]
                dst = dst.rearrange("p (k f) -> p k f", k=KD)
            elif u < M_OUT // 2:
                c, kk = CHUNK_COL[CHUNKS[(u - 6) // 2]], 4 * ((u - 6) % 2)
                src = w_in.rearrange("(k p) f -> p k f", p=P)[:, kk:kk + 4, c:c + 512]
                dst = dst.rearrange("p (k f) -> p k f", k=4)
            else:
                r = OUT_ROWS[2 * (u - M_OUT // 2)]
                src = w_out.rearrange("(t p) d -> p t d", p=P)[:, r:r + 2, :]
                dst = dst.rearrange("p (t d) -> p t d", t=2)
            eng.dma_start(dst, src).then_inc(raw_loaded[s], 16)

        @block.sync
        def _(sp):
            for t in range(TT):
                sp.dma_start(x[:, t, :], x_in[t * P:(t + 1) * P, :]).then_inc(x_loaded, 16)
            for n in range(2):
                for kind in range(3):
                    if n == 1:
                        u = MIX_UNITS - 3 + kind
                        sp.wait_ge(half_ready, MIX_HALF0 + 2 * u + 2)
                    ffn_load(sp, n, 0, kind)
                with sp.Fori(1, FI) as i:
                    for kind in range(3):
                        sp.wait_ge(half_ready, i * 6 + (FFN_HALF0[n] - 6 + 3 + kind + 1))
                        ffn_load(sp, n, i, kind)
                if n == 0:
                    for u in range(MIX_UNITS):
                        sp.wait_ge(half_ready, MIX_HALF0 - 3 + u + 1 if u < 3 else MIX_HALF0 + 2 * (u - 3) + 2)
                        mix_load(sp, u)
            for t in range(TT):
                sp.wait_ge(final_ready, t + 1)
                sp.dma_start(out[t * P:(t + 1) * P, :], normed[:, t, 0:D]).then_inc(out_stored, 16)
            sp.wait_ge(out_stored, 16 * TT)

        @block.gpsimd
        def _(pool):
            steps = [0]

            def step(ins):
                steps[0] += 1
                ins.then_inc(pool_step, 1)
                pool.wait_ge(pool_step, steps[0])

            pool.dma_start(norm_w[:, 1, :], norms[1].partition_broadcast(P)).then_inc(norm_loaded[1], 16)
            pool.dma_start(mix_w[:, 0:D_ATTN], attn_norm.partition_broadcast(P)).then_inc(params_loaded, 16)
            pool.dma_start(mix_w[:, D_ATTN:], ssd_norm.partition_broadcast(P)).then_inc(params_loaded, 16)
            for j, v in enumerate((D_skip, dt_bias, A_log)):
                pool.dma_start(small[:, j, :], v.partition_broadcast(P)).then_inc(params_loaded, 16)
            pool.dma_start(conv_rows[0:TAPS * CT, :], conv_w.rearrange("k (c p) -> (k c) p", p=P)).then_inc(params_loaded, 16)
            pool.dma_start(conv_rows[TAPS * CT:, :], conv_b.rearrange("(c p) -> c p", p=P)).then_inc(params_loaded, 16)
            pool.dma_start(wdt[:, :, :], w_in[:, D_IN - SH:D_IN].rearrange("(k p) f -> p k f", p=P)).then_inc(params_loaded, 16)
            step(pool.memset(minus_half[:, :], -0.5))

            def rsqrt(n, width):
                pool.wait_ge(sq_ready, n + 1)
                step(pool.tensor_scalar(sumsq[:, n:n + 1], sumsq[:, n:n + 1], 1.0 / width, EPS, ALU.mult, ALU.add))
                pool.tensor_tensor(rstd[:, n:n + 1], sumsq[:, n:n + 1], minus_half[:, :], ALU.pow).then_inc(rstd_ready, 1)

            def rotate(tok):
                v = tok[:, :, :].rearrange("p t (h d) -> p t h d", h=HEADS)
                for t in range(TT):
                    r = v[:, t, :, 0:ROT]
                    sn = sin_t[:, t, :].unsqueeze(1).to_broadcast([P, HEADS, ROT])
                    cs = cos_t[:, t, :].unsqueeze(1).to_broadcast([P, HEADS, ROT])
                    hr = ROT // 2
                    pool.tensor_tensor(rot_t[:, t, :, 0:hr], r[:, :, hr:ROT], sn[:, :, 0:hr], ALU.mult)
                    step(pool.tensor_tensor(rot_t[:, t, :, hr:ROT], r[:, :, 0:hr], sn[:, :, hr:ROT], ALU.mult))
                    step(pool.tensor_tensor(r, r, cs, ALU.mult))
                    pool.tensor_tensor(r, r, rot_t[:, t, :, :], ALU.add).then_inc(rotated, 1)

            for t in range(TT):
                rsqrt(t, D)
            for t in range(TT):
                rsqrt(2 + t, D)
            pool.wait_ge(scaled, 2)
            pool.dma_start(norm_w[:, 0, :], norms[2].partition_broadcast(P)).then_inc(norm_loaded[2], 16)
            pool.wait_ge(scaled, 4)
            pool.dma_start(norm_w[:, 1, :], norms[3].partition_broadcast(P)).then_inc(norm_loaded[3], 16)
            pool.wait_ge(transposed, 8)
            for t in range(TT):
                for j in range(2):
                    pool.wait_ge(x_tok_ready, 2 * j + t + 1)
                    pool.tensor_tensor(
                        normed[:, t, D_ATTN + j * 512:D_ATTN + (j + 1) * 512].rearrange("p (h d) -> p h d", d=SP_),
                        x_tok[:, t, j * 512:(j + 1) * 512].rearrange("p (h d) -> p h d", d=SP_),
                        skip16[:, 8 * j:8 * j + 8].unsqueeze(2).to_broadcast([P, 8, SP_]), ALU.mult).then_inc(skip_ready, 1)
            pool.wait_ge(consts_loaded, 16)
            pool.wait_ge(proj_out, 6)
            rotate(q_tok)
            for t in range(TT):
                rsqrt(4 + t, 512)
            pool.wait_ge(proj_out, 8)
            rotate(k_tok)
            for t in range(TT):
                rsqrt(6 + t, 512)
            for t in range(TT):
                rsqrt(8 + t, 512)
            for t in range(TT):
                pass
            for n in (2, 3):
                for t in range(TT):
                    c = t if n == 2 else 2 + t
                    pool.wait_ge(sq_ready, 10 + 2 * (n - 2) + t + 1)
                    step(pool.tensor_scalar(sumsq[:, c:c + 1], sumsq[:, c:c + 1], 1.0 / D, EPS, ALU.mult, ALU.add))
                    pool.tensor_tensor(rstd[:, c:c + 1], sumsq[:, c:c + 1], minus_half[:, :], ALU.pow).then_inc(rstd_ready, 1)

        @block.scalar
        def _(act):
            def split_hi(h, slot, src, unit, like_cols):
                act.wait_ge(unit[0], unit[1])
                dst = w_hi[:, slot, :]
                act.activation(by_tile(dst) if like_cols else dst, src, ACT.Copy).then_inc(hi_ready, 1)

            def ffn_hi(n, i, odd, kind):
                h, slot, src = ffn_half(n, i, odd, kind)
                u0 = FFN_UNIT0[n] + kind
                split_hi(h, slot, src, (raw_loaded[u0 % RAW_SLOTS], i * 16 + 16 * (u0 // RAW_SLOTS + 1)), kind < 2)

            def mix_hi(m):
                if m >= HALF_SLOTS:
                    act.wait_ge(half_used, m - HALF_SLOTS + 1)
                h, slot, src = mix_half(m)
                u = MIX_UNIT0 + m // 2
                split_hi(h, slot, src, (raw_loaded[u % RAW_SLOTS], 16 * (u // RAW_SLOTS + 1)), m < 12)

            def square(n, src, dst, width):
                act.activation(dst, src, ACT.Square, accum_out=sumsq[:, n:n + 1]).then_inc(sq_ready, 1)

            def norm_stage(n):
                for t in range(TT):
                    if n:
                        act.wait_ge(x_ready, 4 * (n - 1) + 2 * (t + 1))
                    else:
                        act.wait_ge(x_loaded, 32)
                    c = 2 * (n % 2) + t
                    square(c, x[:, t, :], normed[:, t, 0:D], D)
                if n == 3:
                    return
                for t in range(TT):
                    for j in range(2):
                        act.wait_ge(transposed, hT_count(n) + 2 * t + j + 1)
                        act.activation(hT_hi[:, 4 * j:4 * j + 4, t * P:(t + 1) * P],
                                       bank[:, T_BANKS[t][j], :].rearrange("p (k c) -> p k c", k=4),
                                       ACT.Copy).then_inc(hT_hi_ready, 1)

            def ffn_gate(n, i, odd, before, after):
                f = FT * n + 2 * i + odd
                before()
                act.wait_ge(gate_done, f + 1)
                act.activation(silu_g[:, :], bank[:, G_BANK, 0:SEQ], ACT.Silu).then_inc(silu_ready, 1)
                act.wait_ge(gu_ready, f + 1)
                act.activation(gu_hi[:, odd, :], gu[:, :], ACT.Copy).then_inc(gu_hi_ready, 1)
                if not (isinstance(i, int) and i + odd == 0):
                    act.wait_ge(down_done, (FT - 1) * n + 2 * i + odd)
                after()

            def ffn(n, last_before, last_after):
                def step(i, odd):
                    i2, odd2 = (i, 1) if not odd else (i + 1, 0)
                    ffn_gate(n, i, odd, lambda: (ffn_hi(n, i2, odd2, 0), ffn_hi(n, i2, odd2, 1)),
                             lambda: ffn_hi(n, i2, odd2, 2))
                if n == 1:
                    def ahead():
                        for kind in range(2):
                            if kind == 1:
                                act.wait_ge(half_used, 43)
                            ffn_hi(1, 0, 1, kind)
                    ffn_gate(1, 0, 0, ahead, lambda: ffn_hi(1, 0, 1, 2))
                    step(0, 1)
                else:
                    step(0, 0)
                    step(0, 1)
                with act.Fori(1, FI - 1) as i:
                    step(i, 0)
                    step(i, 1)
                step(FI - 1, 0)
                ffn_gate(n, FI - 1, 1, last_before, last_after)

            act.dma_start(cst[:, :], consts).then_inc(consts_loaded, 16)
            act.dma_start(norm_w[:, 0, :], norms[0].partition_broadcast(P)).then_inc(norm_loaded[0], 16)
            for t in range(TT):
                act.wait_ge(x_loaded, 16 * TT)
                square(t, x[:, t, :], normed[:, t, 0:D], D)
            for kind in range(2):
                ffn_hi(0, 0, 0, kind)
            act.wait_ge(consts_loaded, 16)
            act.activation(ident_r[:, :], ident, ACT.Copy).then_inc(consts_r, 1)
            act.activation(mask_r[:, :], cst[:, C_MASK:C_MASK + P], ACT.Copy).then_inc(consts_r, 1)
            for t in range(TT):
                for j in range(2):
                    act.wait_ge(transposed, 2 * t + j + 1)
                    act.activation(hT_hi[:, 4 * j:4 * j + 4, t * P:(t + 1) * P],
                                   bank[:, T_BANKS[t][j], :].rearrange("p (k c) -> p k c", k=4),
                                   ACT.Copy).then_inc(hT_hi_ready, 1)
            ffn_hi(0, 0, 0, 2)
            act.wait_ge(params_loaded, 16 * 8)
            act.activation(wdt_hi[:, :, :], wdt[:, :, :], ACT.Copy).then_inc(wdt_hi_ready, 1)
            act.wait_ge(conv_rows_T, 1)
            act.activation(conv_p[:, :, :], bank[:, 7, 0:(TAPS + 1) * CT].rearrange("p (k c) -> p k c", c=CT),
                           ACT.Copy).then_inc(conv_p_ready, 1)
            act.activation(small[:, 2, :], alog16, ACT.Exp).then_inc(neg_a_ready, 1)

            ffn(0, lambda: (mix_hi(0), mix_hi(1)), lambda: mix_hi(2))
            mix_hi(3)
            mix_hi(4)
            norm_stage(1)
            mix_hi(5)

            act.wait_ge(dt_arg, 1)
            act.activation(dts[:, 2, :, :], dts[:, 1, :, :], ACT.Exp).then_inc(dt_exp, 1)

            def first_tap(j):
                act.wait_ge(half_used, j + 1)
                if j == 0:
                    act.wait_ge(conv_p_ready, 1)
                if j >= 2:
                    act.wait_ge(xbc_ready, j - 1)
                c = CONV_ORDER[j]
                act.activation(conv_acc[:, j % 2, :], bank[:, j % 4, 0:SEQ], ACT.Identity,
                               bias=conv_p[:, TAPS, c:c + 1], scale=conv_p[:, TAPS - 1, c:c + 1]).then_inc(tap_ready, 1)

            def conv_silu(j):
                act.wait_ge(taps_done, j + 1)
                act.activation(xbc[:, CONV_ORDER[j], :], conv_acc[:, j % 2, :], ACT.Silu).then_inc(xbc_ready, 1)

            for j in range(12):
                first_tap(j)
                mix_hi(6 + j)
                conv_silu(j)
                if j == 5:
                    for g in range(GROUPS):
                        act.wait_ge(cb_done, g + 1)
                        act.activation(cb[:, g, :], bank[:, 4 + g, 0:384], ACT.Copy).then_inc(cb_ready, 1)
                if j == 11:
                    for t in range(TT):
                        act.wait_ge(xT_done, t + 1)
                        act.activation(x_tok[:, t, 0:512], bank[:, 6 + t, :], ACT.Copy).then_inc(x_tok_ready, 1)

            def chunk_out(c, func, dst, halves):
                m = M_CHUNK[c]
                for t in range(TT):
                    act.wait_ge(half_used, m + 4)
                    act.activation(dst[:, t, :], bank[:, chunk_bank(c) + t, :], func).then_inc(proj_out, 1)

            mix_hi(18)
            for t in range(TT):
                act.wait_ge(xT_done, TT + t + 1)
                act.activation(x_tok[:, t, 512:1024], bank[:, 6 + t, :], ACT.Copy).then_inc(x_tok_ready, 1)
            mix_hi(19)
            chunk_out("z0", ACT.Silu, z_silu[:, :, 0:512], ())
            for m in (20, 21, 22, 23):
                mix_hi(m)
            chunk_out("z1", ACT.Silu, z_silu[:, :, 512:1024], ())

            def decay_exp(h):
                act.wait_ge(bc_done, h + 1)
                if h >= 2:
                    act.wait_ge(m_ready, 2 * (h - 1))
                for s, (a, b) in enumerate(((0, 256), (256, 384))):
                    act.activation(decay[:, h % 2, a:b], bank[:, 4 + h % 2, a:b], ACT.Exp,
                                   bias=dts[:, 7, s, h:h + 1]).then_inc(decay_ready, 1)

            def squares(base, lo_col, count):
                for t in range(TT):
                    act.wait_ge(gated, count + t + 1)
                    act.activation(x_tok[:, t, lo_col:lo_col + 512] if False else sq_dump(base)[:, t, :],
                                   normed[:, t, lo_col:lo_col + 512], ACT.Square,
                                   accum_out=sumsq[:, base + t:base + t + 1]).then_inc(sq_ready, 1)

            def sq_dump(base):
                return xbc[:, 0:4, :].rearrange("p (t c) s -> p t (c s)", t=TT)

            def mix_hi_T(count, banks, row):
                for t in range(TT):
                    act.wait_ge(transposed, count + t + 1)
                    act.activation(hT_hi[:, row:row + 4, t * P:(t + 1) * P],
                                   bank[:, banks[t], :].rearrange("p (k c) -> p k c", k=4),
                                   ACT.Copy).then_inc(hT_hi_ready, 1)

            for j in range(8):
                decay_exp(2 * j)
                decay_exp(2 * j + 1)
                mix_hi(24 + j)
                if j == 4:
                    chunk_out("q", ACT.Copy, q_tok, ())
                if j == 6:
                    squares(4, D_ATTN, 0)
            mix_hi_T(8, (0, 1), 8)
            chunk_out("k", ACT.Copy, k_tok, ())
            mix_hi(32)
            for t in range(TT):
                act.wait_ge(qkT_done, t + 1)
                act.activation(qT[:, :, t * P:(t + 1) * P], bank[:, 4 + t, :].rearrange("p (k c) -> p k c", k=4),
                               ACT.Copy).then_inc(qkT_ready, 1)
            mix_hi(33)
            squares(6, D_ATTN + 512, 2)
            for t in range(TT):
                act.wait_ge(qkT_done, TT + t + 1)
                act.activation(kT[:, :, t * P:(t + 1) * P], bank[:, 6 + t, :].rearrange("p (k c) -> p k c", k=4),
                               ACT.Copy).then_inc(qkT_ready, 1)
            mix_hi(34)

            def softmax_exp(h):
                act.wait_ge(max_ready, h + 1)
                if h >= 2:
                    act.wait_ge(probsT_done, h - 1)
                for t, (a, b) in enumerate(((0, 128), (128, 384))):
                    act.activation(probs[:, h % 2, a:b], bank[:, score_bank(h), a:b], ACT.Exp,
                                   bias=row_bias[:, h, t:t + 1], scale=HD ** -0.5,
                                   accum_out=row_sum[:, t, h:h + 1]).then_inc(probs_ready, 1)

            def probsT_out(h):
                act.wait_ge(probsT_done, h + 1)
                if h >= 2:
                    act.wait_ge(pv_done, h - 1)
                act.activation(probsT[:, h % 2, :], bank[:, score_bank(h) + 1, 0:384], ACT.Copy).then_inc(probsT_ready, 1)

            softmax_exp(0)
            softmax_exp(1)
            mix_hi(35)
            probsT_out(0)
            probsT_out(1)
            softmax_exp(2)
            softmax_exp(3)
            chunk_out("v", ACT.Copy, v_tok, ())
            mix_hi(36)
            probsT_out(2)
            probsT_out(3)
            mix_hi_T(10, (2, 3), 0)
            softmax_exp(4)
            mix_hi(37)
            for h in range(4, 8):
                probsT_out(h)
                if h < 7:
                    softmax_exp(h + 1)
                mix_hi(34 + h)
            squares(8, 0, 4)
            mix_hi(42)
            mix_hi(43)
            for kind in range(2):
                act.wait_ge(half_used, 39 + kind)
                ffn_hi(1, 0, 0, kind)
            mix_hi_T(12, (4, 5), 4)
            act.wait_ge(half_used, 41)
            ffn_hi(1, 0, 0, 2)
            act.wait_ge(half_used, 42)
            norm_stage(2)
            ffn(1, lambda: None, lambda: None)
            norm_stage(3)

        @block.vector
        def _(dve):
            steps = [0]

            def step(ins):
                steps[0] += 1
                ins.then_inc(dve_step, 1)
                dve.wait_ge(dve_step, steps[0])

            def split_lo(h, slot, src, like_cols):
                dve.wait_ge(hi_ready, h + 1)
                hi, lo = w_hi[:, slot, :].bitcast(f32), w_lo[:, slot, :]
                if like_cols:
                    hi, lo = by_tile(hi), by_tile(lo)
                dve.tensor_tensor(lo, src, hi, ALU.subtract).then_inc(half_ready, 1)

            def ffn_lo(n, i, odd, kind):
                h, slot, src = ffn_half(n, i, odd, kind)
                split_lo(h, slot, src, kind < 2)

            def mix_lo(m):
                h, slot, src = mix_half(m)
                split_lo(h, slot, src, m < 12)

            def update_x(n):
                for t in range(TT):
                    dve.wait_ge(acc_ready, TT * (n - 1) + t + 1)
                    for c in range(2):
                        xs = x[:, t, c * 512:(c + 1) * 512]
                        dve.scalar_tensor_tensor(xs, bank[:, 2 * t + c, :], 1.0 if n == 2 else 0.5, xs,
                                                 ALU.mult, ALU.add).then_inc(x_ready, 1)

            def scale_x(n):
                dve.wait_ge(norm_loaded[n], 16)
                for t in range(TT):
                    c = 2 * (n % 2) + t
                    dve.wait_ge(rstd_ready, (0, 2, 10, 12)[n] + t + 1)
                    dve.scalar_tensor_tensor(normed[:, t, 0:D], x[:, t, :], rstd[:, c:c + 1], norm_w[:, n % 2, :],
                                             ALU.mult, ALU.mult).then_inc(final_ready if n == 3 else scaled, 1)

            def hT_lo_part(count, bank_n, row, t):
                dve.wait_ge(hT_hi_ready, count)
                part = slice(t * P, (t + 1) * P)
                dve.tensor_tensor(hT_lo[:, row:row + 4, part],
                                  bank[:, bank_n, :].rearrange("p (k c) -> p k c", k=4),
                                  hT_hi[:, row:row + 4, part].bitcast(f32), ALU.subtract).then_inc(hT_ready, 1)

            def norm_stage(n):
                if n:
                    update_x(n)
                scale_x(n)
                if n < 3:
                    for t in range(TT):
                        for j in range(2):
                            hT_lo_part(hT_count(n) + 2 * t + j + 1, T_BANKS[t][j], 4 * j, t)

            def ffn_up(n, i, odd, before, after):
                f = FT * n + 2 * i + odd
                before()
                dve.wait_ge(up_done, f + 1)
                dve.wait_ge(silu_ready, f + 1)
                if not (isinstance(f, int) and f == 0):
                    dve.wait_ge(gu_split, f)
                dve.tensor_tensor(gu[:, :], bank[:, U_BANK, 0:SEQ], silu_g[:, :], ALU.mult).then_inc(gu_ready, 1)
                dve.wait_ge(gu_hi_ready, f + 1)
                dve.tensor_tensor(gu_lo[:, odd, :], gu[:, :], gu_hi[:, odd, :].bitcast(f32),
                                  ALU.subtract).then_inc(gu_split, 1)
                after()

            def ffn(n, last_before, last_after):
                def fstep(i, odd):
                    i2, odd2 = (i, 1) if not odd else (i + 1, 0)
                    ffn_up(n, i, odd, lambda: (ffn_lo(n, i2, odd2, 0), ffn_lo(n, i2, odd2, 1)),
                           lambda: ffn_lo(n, i2, odd2, 2))
                fstep(0, 0)
                fstep(0, 1)
                with dve.Fori(1, FI - 1) as i:
                    fstep(i, 0)
                    fstep(i, 1)
                fstep(FI - 1, 0)
                ffn_up(n, FI - 1, 1, last_before, last_after)

            scale_x(0)
            for kind in range(2):
                ffn_lo(0, 0, 0, kind)
            for t in range(TT):
                for j in range(2):
                    hT_lo_part(2 * t + j + 1, T_BANKS[t][j], 4 * j, t)
            ffn_lo(0, 0, 0, 2)
            dve.wait_ge(wdt_hi_ready, 1)
            dve.tensor_tensor(wdt_lo[:, :, :], wdt[:, :, :], wdt_hi[:, :, :].bitcast(f32),
                              ALU.subtract).then_inc(wdt_ready, 1)
            ffn(0, lambda: (mix_lo(0), mix_lo(1)), lambda: mix_lo(2))
            mix_lo(3)
            mix_lo(4)
            norm_stage(1)
            mix_lo(5)

            v, e, z, w, p, dt, cs, ncs = (dts[:, j, :, :] for j in (0, 2, 3, 4, 5, 6, 1, 7))
            dve.wait_ge(dt_done, 1)
            dve.wait_ge(params_loaded, 16 * 8)
            step(dve.tensor_tensor(v, bank[:, 7, 0:TT * SH].rearrange("p (t h) -> p t h", t=TT),
                                   bias16.unsqueeze(1).to_broadcast([P, TT, SH]), ALU.add))
            dve.scalar_tensor_tensor(dts[:, 1, :, :], v, -1.0, v, ALU.mult, ALU.min).then_inc(dt_arg, 1)

            def softplus_and_cumsum():
                dve.wait_ge(dt_exp, 1)
                step(dve.tensor_scalar(w, e, 2.0, None, ALU.add))
                step(dve.reciprocal(p, w))
                step(dve.tensor_tensor(z, e, p, ALU.mult))
                step(dve.tensor_tensor(w, z, z, ALU.mult))
                step(dve.tensor_scalar(p, w, 1.0 / 15, None, ALU.mult))
                for k in (13, 11, 9, 7, 5, 3):
                    step(dve.scalar_tensor_tensor(p, p, 1.0 / k, w, ALU.add, ALU.mult))
                step(dve.scalar_tensor_tensor(p, p, 1.0, z, ALU.add, ALU.mult))
                step(dve.tensor_scalar(v, v, 0.0, None, ALU.max))
                step(dve.scalar_tensor_tensor(dt, p, 2.0, v, ALU.mult, ALU.add))
                dve.wait_ge(neg_a_ready, 1)
                dve.scalar_tensor_tensor(z, dt, -1.0, alog16.unsqueeze(1).to_broadcast([P, TT, SH]),
                                         ALU.mult, ALU.mult).then_inc(a_ready, 1)

            def cumsum_out():
                dve.wait_ge(cs_done, 1)
                dve.tensor_copy(cs, bank[:, 6, 0:TT * SH].rearrange("p (t h) -> p t h", t=TT)).then_inc(cs_tok_ready, 1)
                dve.wait_ge(cs_tok_ready, 1)
                step(dve.tensor_scalar(ncs, cs, -1.0, None, ALU.mult))
                dve.wait_ge(csT_done, 1)
                step(dve.tensor_copy(csT_hi[:, :], bank[0:SH, 7, 0:SEQ]))
                dve.tensor_tensor(csT_lo[:, :], bank[0:SH, 7, 0:SEQ], csT_hi[:, :].bitcast(f32),
                                  ALU.subtract).then_inc(csT_ready, 1)

            def conv_taps(j):
                dve.wait_ge(tap_ready, j + 1)
                acc, u, c = conv_acc[:, j % 2, :], bank[:, j % 4, :], CONV_ORDER[j]
                for s in (1, 2, 3):
                    ins = dve.scalar_tensor_tensor(acc[:, s:SEQ], u[:, 0:SEQ - s],
                                                   conv_p[:, TAPS - 1 - s, c:c + 1], acc[:, s:SEQ],
                                                   ALU.mult, ALU.add)
                    if s < 3:
                        step(ins)
                    else:
                        ins.then_inc(taps_done, 1)

            for j in range(12):
                conv_taps(j)
                if j == 0:
                    softplus_and_cumsum()
                mix_lo(6 + j)
                if j == 2:
                    cumsum_out()
            for m in (18, 19, 20, 21, 22, 23):
                mix_lo(m)

            def weigh(h):
                g = h // 8
                if h == 0:
                    dve.wait_ge(cb_ready, 2)
                if h >= 2:
                    dve.wait_ge(y_done, h - 1)
                for s, (a, b) in enumerate(((0, 256), (256, 384))):
                    dve.wait_ge(decay_ready, 2 * h + s + 1)
                    dve.scalar_tensor_tensor(mix_m[:, h % 2, a:b], cb[:, g, a:b], dts[:, 6, s, h:h + 1],
                                             decay[:, h % 2, a:b], ALU.mult, ALU.mult).then_inc(m_ready, 1)

            def ssd_gate(g):
                cols = slice(D_ATTN + 512 * g, D_ATTN + 512 * (g + 1))
                dve.wait_ge(y_done, 8 * (g + 1))
                dve.wait_ge(skip_ready, 4)
                for t in range(TT):
                    dve.tensor_tensor(normed[:, t, cols], bank[:, 6 + t, :], normed[:, t, cols], ALU.add).then_inc(y_added, 1)
                for t in range(TT):
                    dve.wait_ge(y_added, 2 * g + t + 1)
                    dve.wait_ge(proj_out, 2 * (g + 1))
                    dve.tensor_tensor(normed[:, t, cols], normed[:, t, cols], z_silu[:, t, 512 * g:512 * (g + 1)],
                                      ALU.mult).then_inc(gated, 1)

            def mix_scale(base, cols, count):
                for t in range(TT):
                    dve.wait_ge(rstd_ready, count + t + 1)
                    dve.scalar_tensor_tensor(normed[:, t, cols], normed[:, t, cols], rstd[:, base + t:base + t + 1],
                                             mix_w[:, cols], ALU.mult, ALU.mult).then_inc(scaled, 1)

            for j in range(8):
                weigh(2 * j)
                weigh(2 * j + 1)
                mix_lo(24 + j)
                if j == 4:
                    ssd_gate(0)
                if j == 6:
                    mix_scale(4, slice(D_ATTN, D_ATTN + 512), 4)
            for t in range(TT):
                hT_lo_part(8 + t + 1, t, 8, t)
            ssd_gate(1)
            mix_lo(32)
            mix_lo(33)
            mix_scale(6, slice(D_ATTN + 512, D_MIX), 6)
            mix_lo(34)

            def score_max(h):
                dve.wait_ge(scores_done, h + 1)
                dve.reduce_max(row_max[:, h, 0:1], bank[:, score_bank(h), 0:128], axis=AX.X)
                step(dve.reduce_max(row_max[:, h, 1:2], bank[:, score_bank(h), 128:384], axis=AX.X))
                dve.tensor_scalar(row_bias[:, h, :], row_max[:, h, :], -(HD ** -0.5), None, ALU.mult).then_inc(max_ready, 1)

            score_max(0)
            score_max(1)
            mix_lo(35)
            score_max(2)
            score_max(3)
            mix_lo(36)
            for t in range(TT):
                hT_lo_part(10 + t + 1, 2 + t, 0, t)
            score_max(4)
            mix_lo(37)
            for h in range(4, 8):
                if h < 7:
                    score_max(h + 1)
                mix_lo(34 + h)
            dve.wait_ge(probs_ready, 2 * HEADS)
            step(dve.reciprocal(row_inv[:, :, :], row_sum[:, :, :]))
            dve.wait_ge(pv_done, HEADS)
            for t in range(TT):
                dve.tensor_tensor(normed[:, t, 0:D_ATTN].rearrange("p (h d) -> p h d", d=HD),
                                  bank[:, 6 + t, :].rearrange("p (h d) -> p h d", d=HD),
                                  row_inv[:, t, :].unsqueeze(2).to_broadcast([P, HEADS, HD]), ALU.mult).then_inc(gated, 1)
            mix_scale(8, slice(0, D_ATTN), 8)
            mix_lo(42)
            mix_lo(43)
            for kind in range(2):
                ffn_lo(1, 0, 0, kind)
            for t in range(TT):
                hT_lo_part(12 + t + 1, 4 + t, 4, t)
            ffn_lo(1, 0, 0, 2)
            norm_stage(2)
            ffn(1, lambda: None, lambda: None)
            norm_stage(3)

        @block.tensor
        def _(pe):
            def three(dst, lhs, rhs, start, stop):
                pe.matmul(dst, lhs[0], rhs[0], start=start, stop=False, skip_group_check=True)
                pe.matmul(dst, lhs[0], rhs[1], start=False, stop=False, skip_group_check=True)
                return pe.matmul(dst, lhs[1], rhs[0], start=False, stop=stop, skip_group_check=True)

            def hT(k, part):
                return hT_hi[:, k, part], hT_lo[:, k, part]

            def w_cols(slot, k):
                return tuple(w[:, slot, k * P:(k + 1) * P] for w in (w_hi, w_lo))

            def tok(t):
                return slice(t * P, (t + 1) * P)

            def columns_product(slot, dst, done):
                for k in range(KD):
                    last = three(dst, w_cols(slot, k), hT(k, slice(0, SEQ)), k == 0, k == KD - 1)
                last.then_inc(done, 1)

            def down(n, i, odd, t, start, stop, done=None):
                h, slot, _ = ffn_half(n, i, odd, 2)
                for c in range(2):
                    last = three(bank[:, 2 * t + c, :], (gu_hi[:, odd, tok(t)], gu_lo[:, odd, tok(t)]),
                                 tuple(w[:, slot, c * 512:(c + 1) * 512] for w in (w_hi, w_lo)), start, stop)
                if done is not None:
                    last.then_inc(done, 1)

            def down_both(n, i, odd, start):
                down(n, i, odd, 0, start, False)
                down(n, i, odd, 1, start, False, down_done)

            def down_waits(n, i, odd):
                pe.wait_ge(half_ready, ffn_half(n, i, odd, 2)[0] + 1)
                pe.wait_ge(gu_split, FT * n + 2 * i + odd + 1)

            def gate_up(n, i, odd):
                f = FT * n + 2 * i + odd
                for kind, dst, done, free in ((0, G_BANK, gate_done, silu_ready), (1, U_BANK, up_done, gu_ready)):
                    h, slot, _ = ffn_half(n, i, odd, kind)
                    pe.wait_ge(half_ready, h + 1)
                    if not (isinstance(f, int) and f == 0):
                        pe.wait_ge(free, f)
                    columns_product(slot, bank[:, dst, 0:SEQ], done)

            def ffn(n):
                pe.wait_ge(hT_ready, hT_count(2 * n) + 4)
                gate_up(n, 0, 0)
                gate_up(n, 0, 1)
                if n:
                    pe.wait_ge(x_ready, 8)
                down_waits(n, 0, 0)
                down_both(n, 0, 0, True)
                with pe.Fori(1, FI - 1) as i:
                    gate_up(n, i, 0)
                    down_waits(n, i - 1, 1)
                    down_both(n, i - 1, 1, False)
                    gate_up(n, i, 1)
                    down_waits(n, i, 0)
                    down_both(n, i, 0, False)
                i = FI - 1
                gate_up(n, i, 0)
                down_waits(n, i - 1, 1)
                down_both(n, i - 1, 1, False)
                gate_up(n, i, 1)
                down_waits(n, i, 0)
                down(n, i, 0, 0, False, False)
                down_waits(n, i, 1)
                down(n, i, 1, 0, False, True, acc_ready)
                down(n, i, 0, 1, False, False, down_done)
                down(n, i, 1, 1, False, True, acc_ready)

            def transpose_rows(t, col, bank_n):
                for k in range(4):
                    last = pe.transpose(bank[:, bank_n, k * P:(k + 1) * P],
                                        normed[:, t, col + k * P:col + (k + 1) * P], ident)
                last.then_inc(transposed, 1)

            def norm_transposes(n):
                for t in range(TT):
                    pe.wait_ge(scaled, (0, 2, 10)[n] + t + 1)
                    for j in range(2):
                        transpose_rows(t, 512 * j, T_BANKS[t][j])

            pe.wait_ge(consts_loaded, 16)
            norm_transposes(0)
            pe.wait_ge(params_loaded, 16 * 8)
            pe.wait_ge(hT_ready, 4)
            pe.transpose(bank[:, 7, 0:(TAPS + 1) * CT], conv_rows[:, :],
                         cst[0:(TAPS + 1) * CT, C_ID:C_ID + (TAPS + 1) * CT]).then_inc(conv_rows_T, 1)
            ffn(0)
            norm_transposes(1)

            pe.wait_ge(hT_ready, 8)
            pe.wait_ge(wdt_ready, 1)
            for t in range(TT):
                for k in range(KD):
                    last = three(bank[:, 7, t * SH:(t + 1) * SH], hT(k, tok(t)),
                                 (wdt_hi[:, k, :], wdt_lo[:, k, :]), k == 0, k == KD - 1)
            last.then_inc(dt_done, 1)

            def conv_half(j):
                pe.wait_ge(half_ready, MIX_HALF0 + j + 1)
                if j >= 4:
                    pe.wait_ge(taps_done, j - 3)
                columns_product(mix_half(j)[1], bank[:, j % 4, 0:SEQ], half_used)

            def cumsum():
                pe.wait_ge(a_ready, 1)
                a = dts[:, 3, :, :]
                pe.matmul(bank[:, 6, 0:SH], tri[:, 0:P], a[:, 0, :], start=True, stop=True)
                pe.matmul(bank[:, 6, SH:2 * SH], tri[:, P:SEQ], a[:, 0, :], start=True, stop=False)
                pe.matmul(bank[:, 6, SH:2 * SH], tri[:, 0:P], a[:, 1, :], start=False, stop=True).then_inc(cs_done, 1)

            def cumsum_T():
                pe.wait_ge(cs_tok_ready, 1)
                for t in range(TT):
                    last = pe.transpose(bank[0:SH, 7, tok(t)], dts[:, 1, t, :], ident)
                last.then_inc(csT_done, 1)

            def cb_products():
                pe.wait_ge(xbc_ready, 4)
                for g in range(GROUPS):
                    b, c = xbc[:, 8 + g, :], xbc[:, 10 + g, :]
                    pe.matmul(bank[:, 4 + g, 0:SEQ], b[:, 0:P], c, start=True, stop=True)
                    pe.matmul(bank[:, 4 + g, SEQ:SEQ + P], b[:, P:SEQ], c[:, P:SEQ], start=True, stop=True).then_inc(cb_done, 1)

            def x_transposes(j):
                pe.wait_ge(xbc_ready, 4 + 4 * (j + 1))
                if j == 1:
                    pe.wait_ge(x_tok_ready, 2)
                else:
                    pe.wait_ge(csT_ready, 1)
                for t in range(TT):
                    for k in range(4):
                        last = pe.transpose(bank[:, 6 + t, k * P:(k + 1) * P], xbc[:, 4 * j + k, tok(t)], ident)
                    last.then_inc(xT_done, 1)

            def chunk_half(m):
                c, q = CHUNKS[(m - 12) // 4], (m - 12) % 4
                b = chunk_bank(c)
                slot = mix_half(m)[1]
                pe.wait_ge(half_ready, MIX_HALF0 + m + 1)
                if q == 0:
                    for need in chunk_needs(c):
                        pe.wait_ge(*need)
                for t in range(TT):
                    for k in range(2):
                        last = three(bank[:, b + t, :], hT(2 * q + k, tok(t)),
                                     tuple(w[:, slot, k * 512:(k + 1) * 512] for w in (w_hi, w_lo)),
                                     q == 0 and k == 0, q == 3 and k == 1)
                last.then_inc(half_used, 1)

            def chunk_needs(c):
                return {"z0": [(taps_done, 10)], "z1": [(taps_done, 12)], "q": [(proj_out, 2)],
                        "k": [(proj_out, 4)], "v": [(proj_out, 6), (hT_ready, 10)]}[c]

            def decay_args(h):
                b = bank[:, 4 + h % 2, :]
                if h >= 2:
                    pe.wait_ge(decay_ready, 2 * (h - 1))
                else:
                    pe.wait_ge(cb_ready, 2)
                    pe.wait_ge(csT_ready, 1)
                    pe.wait_ge(consts_r, 2)
                head = ident_r[0:SH, h:h + 1].to_broadcast([SH, P])
                first = True
                for a, c, lo in ((0, SEQ, 0), (SEQ, SEQ + P, P)):
                    for part in (csT_hi, csT_lo):
                        pe.matmul(b[:, a:c], head, part[:, lo:SEQ], start=first, stop=False, skip_group_check=True)
                        first = False
                for a in (0, SEQ):
                    last = pe.matmul(b[:, a:a + P], ident_r[:, :], mask_r[:, :], start=False, stop=a > 0,
                                     skip_group_check=True)
                last.then_inc(bc_done, 1)

            def ssd_out(h):
                pe.wait_ge(m_ready, 2 * (h + 1))
                if h == 0:
                    pe.wait_ge(x_tok_ready, 4)
                if h == 8:
                    pe.wait_ge(y_added, 2)
                m, c, o = mix_m[:, h % 2, :], slice(h * SP_, (h + 1) * SP_), slice((h % 8) * SP_, (h % 8 + 1) * SP_)
                pe.matmul(bank[:, 6, o], m[:, 0:P], x_tok[:, 0, c], start=True, stop=True)
                pe.matmul(bank[:, 7, o], m[:, P:SEQ], x_tok[:, 0, c], start=True, stop=False)
                pe.matmul(bank[:, 7, o], m[:, SEQ:SEQ + P], x_tok[:, 1, c], start=False, stop=True).then_inc(y_done, 1)

            def mix_transposes(count, col, banks, need=()):
                for n in need:
                    pe.wait_ge(*n)
                for t in range(TT):
                    pe.wait_ge(scaled, count + t + 1)
                    transpose_rows(t, col, banks[t])

            def qk_transposes(tensor, bank0, count):
                pe.wait_ge(rotated, count)
                for t in range(TT):
                    for k in range(4):
                        last = pe.transpose(bank[:, bank0 + t, k * P:(k + 1) * P], tensor[:, t, k * P:(k + 1) * P], ident)
                    last.then_inc(qkT_done, 1)

            def scores(h):
                r, p, b = slice(HD * (h % 2), HD * (h % 2 + 1)), h // 2, bank[:, score_bank(h), :]
                if h == 0:
                    pe.wait_ge(qkT_ready, 4)
                if h == 1:
                    pe.wait_ge(proj_out, 8)
                if h >= 2:
                    pe.wait_ge(probs_ready, 2 * (h - 1) if h < 5 else 2 * h)
                pe.matmul(b[:, 0:P], qT[r, p, 0:P], kT[r, p, 0:P], start=True, stop=False, skip_group_check=True)
                pe.matmul(b[:, P:P + SEQ], qT[r, p, P:SEQ], kT[r, p, :], start=False, stop=False, skip_group_check=True)
                for a in (0, SEQ):
                    last = pe.matmul(b[:, a:a + P], mask_r[:, :], ident_r[:, :], start=False, stop=a > 0,
                                     skip_group_check=True)
                last.then_inc(scores_done, 1)

            def probs_transposes(h):
                pe.wait_ge(probs_ready, 2 * (h + 1))
                if h >= 2:
                    pe.wait_ge(probsT_ready, h - 1 if h < 5 else h)
                for a in range(3):
                    last = pe.transpose(bank[:, score_bank(h) + 1, a * P:(a + 1) * P],
                                        probs[:, h % 2, a * P:(a + 1) * P], ident)
                last.then_inc(probsT_done, 1)

            def pv(h):
                pe.wait_ge(probsT_ready, h + 1)
                if h == 0:
                    pe.wait_ge(proj_out, 10)
                pt, c = probsT[:, h % 2, :], slice(h * HD, (h + 1) * HD)
                pe.matmul(bank[:, 6, c], pt[:, 0:P], v_tok[:, 0, c], start=True, stop=True)
                pe.matmul(bank[:, 7, c], pt[:, P:SEQ], v_tok[:, 0, c], start=True, stop=False)
                pe.matmul(bank[:, 7, c], pt[:, SEQ:SEQ + P], v_tok[:, 1, c], start=False, stop=True).then_inc(pv_done, 1)

            def out_half(j):
                m = M_OUT + j
                slot = mix_half(m)[1]
                pe.wait_ge(half_ready, MIX_HALF0 + m + 1)
                if j % 4 == 0:
                    pe.wait_ge(hT_ready, 10 + 2 * (j // 4))
                if j == 0:
                    pe.wait_ge(proj_out, 10)
                for t in range(TT):
                    if j == 0 and t == 1:
                        pe.wait_ge(hT_ready, 12)
                    for c in range(2):
                        last = three(bank[:, 2 * t + c, :], hT(mix_row(OUT_ROWS[j]), tok(t)),
                                     tuple(w[:, slot, c * 512:(c + 1) * 512] for w in (w_hi, w_lo)),
                                     j == 0, j == 11)
                    if j == 11:
                        last.then_inc(acc_ready, 1)
                if j < 11:
                    last.then_inc(half_used, 1)

            after = {m: [] for m in range(MIX_HALVES)}
            after[1] += [cumsum]
            after[3] += [cumsum_T]
            after[6] += [cb_products]
            after[10] += [lambda: x_transposes(0)]
            after[14] += [lambda: x_transposes(1)]
            after[19] += [lambda: decay_args(0), lambda: decay_args(1)]
            for j in range(8):
                for h in (2 * j, 2 * j + 1):
                    after[20 + j] += [lambda h=h: ssd_out(h)]
                    if h + 2 < SH:
                        after[20 + j] += [lambda h=h: decay_args(h + 2)]
            after[27] += [lambda: mix_transposes(4, D_ATTN, (0, 1), [(proj_out, 6)])]
            after[28] += [lambda: qk_transposes(q_tok, 4, 2)]
            after[29] += [lambda: pe.wait_ge(y_added, 4), lambda: qk_transposes(k_tok, 6, 4)]
            after[29] += [lambda: scores(0), lambda: scores(1)]
            after[30] += [lambda: probs_transposes(0), lambda: probs_transposes(1), lambda: scores(2), lambda: scores(3)]
            after[31] += [lambda: pv(0), lambda: pv(1), lambda: probs_transposes(2), lambda: probs_transposes(3), lambda: scores(4)]
            after[31] += [lambda: mix_transposes(6, D_ATTN + 512, (2, 3), [(probsT_ready, 4)])]
            after[32] += [lambda: pv(2), lambda: pv(3), lambda: probs_transposes(4), lambda: scores(5)]
            for h in range(4, 8):
                after[29 + h] += [lambda h=h: pv(h)]
                if h < 7:
                    after[29 + h] += [lambda h=h: probs_transposes(h + 1)]
                if h < 6:
                    after[29 + h] += [lambda h=h: scores(h + 2)]
            after[39] += [lambda: mix_transposes(8, 0, (4, 5))]

            for m in range(MIX_HALVES):
                if m < 12:
                    conv_half(m)
                elif m < M_OUT:
                    chunk_half(m)
                else:
                    out_half(m - M_OUT)
                for f in after[m]:
                    f()

            norm_transposes(2)
            ffn(1)


def hT_count(n):
    return (0, 4, 14)[n]


def chunk_bank(c):
    return {"z0": 0, "z1": 2, "q": 0, "k": 2, "v": 0}[c]


def score_bank(h):
    return 2 if h in (1, 3) else 4


_INS = ["x", "ffn1_norm", "ffn1_w1", "ffn1_w3", "ffn1_w2", "mix_norm", "w_in", "conv_w", "conv_b",
        "dt_bias", "A_log", "D_skip", "attn_out_norm", "ssd_out_norm", "w_out",
        "ffn2_norm", "ffn2_w1", "ffn2_w3", "ffn2_w2", "final_norm"]


def kernel(**inputs):
    import concourse.bacc as bacc
    from concourse.bass_utils import run_bass_kernel_spmd

    nc = bacc.Bacc("TRN2", target_bir_lowering=False, num_devices=1)
    arrays, t = {}, {}
    for name in _INS + ["shape_constants"]:
        if name == "shape_constants":
            a = shape_constants()
        else:
            a = np.ascontiguousarray(inputs[name])
            if name != "final_norm":
                a = a[0]
        arrays[f"in_{name}"] = a
        t[name] = nc.dram_tensor(f"in_{name}", a.shape, mybir.dt.from_np(a.dtype), kind="ExternalInput").ap()
    out = nc.dram_tensor("out_x", (SEQ, D), mybir.dt.float32, kind="ExternalOutput").ap()
    build(nc, t["x"], (t["ffn1_w1"], t["ffn2_w1"]), (t["ffn1_w3"], t["ffn2_w3"]), (t["ffn1_w2"], t["ffn2_w2"]),
          (t["ffn1_norm"], t["mix_norm"], t["ffn2_norm"], t["final_norm"]), t["w_in"], t["conv_w"], t["conv_b"],
          t["dt_bias"], t["A_log"], t["D_skip"], t["attn_out_norm"], t["ssd_out_norm"], t["w_out"],
          t["shape_constants"], out)
    r = run_bass_kernel_spmd(nc, [arrays], core_ids=[0])
    return r.results[0]["out_x"].reshape(1, SEQ, D)
```

```python
from contextlib import ExitStack

import numpy as np
import concourse.bass as bass
from concourse import mybir

P = 128
SEQ, D, F = 256, 1024, 2816
TT = SEQ // P
KD = D // P
HEADS, HD, ROT = 8, 64, 16
D_ATTN = HEADS * HD
SH, SP_, GROUPS = 16, 64, 2
D_SSM = SH * SP_
N_STATE, TAPS = 128, 4
D_CONV = D_SSM + 2 * GROUPS * N_STATE
D_IN = 3 * D_ATTN + D_SSM + D_CONV + SH
D_MIX = D_ATTN + D_SSM
CT = D_CONV // P
EPS = 1e-6
THETA = 500000.0
MASKED = -(2.0 ** 99)

RAW_SLOTS, HALF_SLOTS = 3, 6
HALF = 1024
FT = F // P
FI = FT // 2

MIX_UNIT0 = 3 * FI
CONV_ORDER = (8, 9, 10, 11, 0, 1, 2, 3, 4, 5, 6, 7)
CHUNKS = ("z0", "q", "k", "z1", "v")
M_CHUNK = {"z0": 0, "q": 16, "k": 20, "z1": 24, "v": 28}
M_CONV, M_OUT = 4, 32
CHUNK_COL = {"q": 0, "k": D_ATTN, "v": 2 * D_ATTN, "z0": 3 * D_ATTN, "z1": 3 * D_ATTN + 512}
OUT_ROWS = (4, 5, 6, 7, 8, 9, 10, 11, 0, 1, 2, 3)
MIX_HALVES = 12 + 4 * len(CHUNKS) + 12
MIX_UNITS = MIX_HALVES // 2
MIX_HALF0 = 6 * FI
FFN_UNIT0 = (0, MIX_UNIT0 + MIX_UNITS)
FFN_HALF0 = (0, MIX_HALF0 + MIX_HALVES)

C_ID, C_TRI, C_MASK, C_COS, C_SIN, C_END = 0, 128, 384, 512, 544, 576

def mix_row(r):
    return {0: 4, 1: 8, 2: 0}[r // 4] + r % 4


def shape_constants():
    c = np.zeros((P, C_END), np.float32)
    c[:, C_ID:C_ID + P] = np.eye(P)
    c[:, C_TRI:C_TRI + P] = np.triu(np.ones((P, P)))
    c[:, C_TRI + P:C_TRI + 2 * P] = 1.0
    c[:, C_MASK:C_MASK + P] = np.where(np.triu(np.ones((P, P))) > 0, 0.0, MASKED)
    inv = (np.float32(THETA) ** (-np.arange(0, ROT, 2, dtype=np.float32) / np.float32(ROT))).astype(np.float32)
    ang = np.arange(SEQ, dtype=np.float32)[:, None] * inv[None, :]
    cos, sin = (f(ang).astype(np.float32).reshape(TT, P, ROT // 2).transpose(1, 0, 2) for f in (np.cos, np.sin))
    c[:, C_COS:C_COS + TT * ROT] = np.concatenate([cos, cos], -1).reshape(P, -1)
    c[:, C_SIN:C_SIN + TT * ROT] = np.concatenate([-sin, sin], -1).reshape(P, -1)
    return c


def build(nc, x_in, w1s, w3s, w2s, norms, w_in, conv_w, conv_b, dt_bias, A_log, D_skip,
          attn_norm, ssd_norm, w_out, consts, out):
    f32, f32r = mybir.dt.float32, mybir.dt.float32r
    ALU, ACT, AX = mybir.AluOpType, mybir.ActivationFunctionType, mybir.AxisListType

    with ExitStack() as ctx:
        def sb(name, shape, dtype=f32):
            return ctx.enter_context(nc.sbuf_tensor(name, shape, dtype))

        def sem(name):
            return ctx.enter_context(nc.semaphore(name))

        raw = sb("raw", [P, RAW_SLOTS, 2 * HALF])
        w_hi = sb("w_hi", [P, HALF_SLOTS, HALF], f32r)
        w_lo = sb("w_lo", [P, HALF_SLOTS, HALF], f32r)
        x = sb("x", [P, TT, D])
        hT_hi = sb("hT_hi", [P, 12, SEQ], f32r)
        hT_lo = sb("hT_lo", [P, 12, SEQ], f32r)
        normed = sb("normed", [P, TT, D_MIX])
        norm_w = sb("norm_w", [P, 2, D])
        mix_w = sb("mix_w", [P, D_MIX])
        cst = sb("cst", [P, C_END])
        ident_r = sb("ident_r", [P, P], f32r)
        mask_r = sb("mask_r", [P, P], f32r)
        small = sb("small", [P, 2, SH])
        conv_rows = sb("conv_rows", [(TAPS + 1) * CT, P])
        conv_p = sb("conv_p", [P, TAPS + 1, CT])
        wdt = sb("wdt", [P, KD, SH])
        wdt_hi = sb("wdt_hi", [P, KD, SH], f32r)
        wdt_lo = sb("wdt_lo", [P, KD, SH], f32r)
        sumsq = sb("sumsq", [P, 2, 10])
        mean_sq = sb("mean_sq", [P, 10])
        rstd = sb("rstd", [P, 10])
        minus_half = sb("minus_half", [P, 1])
        gu = sb("gu", [P, SEQ])
        gu_hi = sb("gu_hi", [P, 2, SEQ], f32r)
        gu_lo = sb("gu_lo", [P, 2, SEQ], f32r)
        bias_col = sb("bias_col", [SH, 1])
        dtT = sb("dtT", [SH, SEQ])
        conv_acc = sb("conv_acc", [P, 4, SEQ])
        silu_g = conv_acc[:, 0, :]
        xbc = sb("xbc", [P, CT, SEQ])
        x_tok = sb("x_tok", [P, TT, D_SSM])
        z_silu = sb("z_silu", [P, TT, D_SSM])
        dts = sb("dts", [P, 8, TT, SH])
        csT_hi = sb("csT_hi", [SH, SEQ], f32r)
        csT_lo = sb("csT_lo", [SH, SEQ], f32r)
        cb = sb("cb", [P, GROUPS, 384])
        decay = sb("decay", [P, 2, 384])
        mix_m = sb("mix_m", [P, 2, 384])
        q_tok = sb("q_tok", [P, TT, D_ATTN])
        k_tok = sb("k_tok", [P, TT, D_ATTN])
        v_tok = sb("v_tok", [P, TT, D_ATTN])
        rot_t = sb("rot_t", [P, TT, HEADS, ROT])
        qT = sb("qT", [P, HEADS // 2, SEQ])
        kT = sb("kT", [P, HEADS // 2, SEQ])
        probs = decay
        probsT = xbc[:, :, :].rearrange("p c l -> p (c l)").rearrange("p (h l) -> p h l", h=HEADS)
        row_max = sb("row_max", [P, HEADS, TT])
        row_bias = sb("row_bias", [P, HEADS, TT])
        row_sum = sb("row_sum", [P, TT, HEADS])
        row_inv = sb("row_inv", [P, TT, HEADS])

        bank = ctx.enter_context(nc.psum_tensor("bank", [P, 8, 512], f32))
        G_BANK, U_BANK = 4, 5
        T_BANKS = (6, 7)

        ident, tri = cst[:, C_ID:C_ID + P], cst[:, C_TRI:C_TRI + SEQ]
        cos_t = cst[:, C_COS:C_COS + TT * ROT].rearrange("p (t r) -> p t r", t=TT)
        sin_t = cst[:, C_SIN:C_SIN + TT * ROT].rearrange("p (t r) -> p t r", t=TT)
        skip16, alog16 = (small[:, j, :] for j in range(2))

        x_loaded = [sem(f"x_loaded{j}") for j in range(2 * TT)]
        ident_loaded = sem("ident_loaded")
        first_loaded = [sem(f"first_loaded{k}") for k in range(3)]
        consts_loaded = sem("consts_loaded")
        params_loaded = sem("params_loaded")
        mix_w_loaded = sem("mix_w_loaded")
        norm_loaded = [sem(f"norm_loaded{n}") for n in range(4)]
        raw_loaded = [sem(f"raw_loaded{s}") for s in range(RAW_SLOTS)]
        hi_ready = sem("hi_ready")
        half_ready = sem("half_ready")
        half_used = sem("half_used")
        consts_r = sem("consts_r")
        wdt_hi_ready = sem("wdt_hi_ready")
        wdt_ready = sem("wdt_ready")
        x_ready = sem("x_ready")
        sq_ready = sem("sq_ready")
        rstd_ready = sem("rstd_ready")
        pool_step = sem("pool_step")
        scaled = sem("scaled")
        transposed = sem("transposed")
        hT_hi_ready = sem("hT_hi_ready")
        hT_ready = sem("hT_ready")
        gate_done = sem("gate_done")
        up_done = sem("up_done")
        down_done = sem("down_done")
        silu_ready = sem("silu_ready")
        gu_ready = sem("gu_ready")
        gu_hi_ready = sem("gu_hi_ready")
        gu_split = sem("gu_split")
        acc_ready = sem("acc_ready")
        dve_step = sem("dve_step")
        neg_a_ready = sem("neg_a_ready")
        conv_rows_T = sem("conv_rows_T")
        conv_p_ready = sem("conv_p_ready")
        dtT_done = sem("dtT_done")
        dtT_ready = sem("dtT_ready")
        dt_done = sem("dt_done")
        z0_first = sem("z0_first")
        dt_arg = sem("dt_arg")
        dt_exp = sem("dt_exp")
        atanh_arg = sem("atanh_arg")
        a_ready = sem("a_ready")
        cs_done = sem("cs_done")
        cs_tok_ready = sem("cs_tok_ready")
        csT_done = sem("csT_done")
        csT_ready = sem("csT_ready")
        tap_ready = sem("tap_ready")
        taps_done = sem("taps_done")
        xbc_ready = sem("xbc_ready")
        cb_done = sem("cb_done")
        cb_ready = sem("cb_ready")
        xT_done = sem("xT_done")
        x_tok_ready = sem("x_tok_ready")
        skip_ready = sem("skip_ready")
        proj_out = sem("proj_out")
        bc_done = sem("bc_done")
        decay_ready = sem("decay_ready")
        m_ready = sem("m_ready")
        y_done = sem("y_done")
        y_added = sem("y_added")
        gated = sem("gated")
        rotated = sem("rotated")
        qkT_done = sem("qkT_done")
        qkT_ready = sem("qkT_ready")
        scores_done = sem("scores_done")
        max_ready = sem("max_ready")
        probs_ready = sem("probs_ready")
        probsT_done = sem("probsT_done")
        probsT_ready = sem("probsT_ready")
        pv_done = sem("pv_done")
        final_ready = sem("final_ready")
        out_stored = sem("out_stored")

        block = ctx.enter_context(nc.Block())

        def cols_half(t, half):
            return t.rearrange("p (k f) -> p k f", k=KD)[:, :, half * P:(half + 1) * P]

        def by_tile(t):
            return t.rearrange("p (k f) -> p k f", k=KD)

        def ffn_half(n, i, odd, kind):
            h0 = FFN_HALF0[n] + 3 * odd + kind
            r = raw[:, (FFN_UNIT0[n] + kind) % RAW_SLOTS, :]
            src = cols_half(r, odd) if kind < 2 else r[:, odd * HALF:(odd + 1) * HALF]
            return h0 + 6 * i, h0 % HALF_SLOTS, src

        def mix_half(m):
            r = raw[:, (MIX_UNIT0 + m // 2) % RAW_SLOTS, :]
            src = cols_half(r, m % 2) if by_columns(m) else r[:, (m % 2) * HALF:(m % 2 + 1) * HALF]
            return MIX_HALF0 + m, (MIX_HALF0 + m) % HALF_SLOTS, src

        def ffn_load(eng, n, i, kind):
            s = (FFN_UNIT0[n] + kind) % RAW_SLOTS
            dst = raw[:, s, :]
            if kind < 2:
                src = (w1s, w3s)[kind][n].rearrange("(k p) f -> p k f", p=P)[:, :, bass.ts(i, 2 * P)]
                dst = dst.rearrange("p (k f) -> p k f", k=KD)
            else:
                src = w2s[n].rearrange("(t p) d -> p t d", p=P)[:, bass.ts(i, 2), :]
                dst = dst.rearrange("p (t d) -> p t d", t=2)
            eng.dma_start(dst, src).then_inc(raw_loaded[s], 16)

        def mix_load(eng, u):
            s = (MIX_UNIT0 + u) % RAW_SLOTS
            dst = raw[:, s, :]
            if by_columns(2 * u):
                c = 3 * D_ATTN + D_SSM + CONV_ORDER[2 * u - M_CONV] * P
                src = w_in.rearrange("(k p) f -> p k f", p=P)[:, :, c:c + 2 * P]
                dst = dst.rearrange("p (k f) -> p k f", k=KD)
            elif u < M_OUT // 2:
                c, kk = CHUNK_COL[chunk_of(2 * u)], 4 * (u % 2)
                src = w_in.rearrange("(k p) f -> p k f", p=P)[:, kk:kk + 4, c:c + 512]
                dst = dst.rearrange("p (k f) -> p k f", k=4)
            else:
                r = OUT_ROWS[2 * (u - M_OUT // 2)]
                src = w_out.rearrange("(t p) d -> p t d", p=P)[:, r:r + 2, :]
                dst = dst.rearrange("p (t d) -> p t d", t=2)
            eng.dma_start(dst, src).then_inc(raw_loaded[s], 16)

        @block.sync
        def _(sp):
            def load_x(t, c):
                cols = slice(c * 512, (c + 1) * 512)
                sp.dma_start(x[:, t, cols], x_in[t * P:(t + 1) * P, cols]).then_inc(x_loaded[2 * t + c], 16)

            load_x(0, 0)
            load_x(0, 1)
            sp.dma_start(cst[:, C_ID:C_ID + P], consts[:, C_ID:C_ID + P]).then_inc(ident_loaded, 16)
            sp.dma_start(norm_w[:, 0, :], norms[0].partition_broadcast(P)).then_inc(norm_loaded[0], 16)
            for odd in range(2):
                for kind in range(3):
                    if odd == 0 and kind == 1:
                        load_x(1, 0)
                        load_x(1, 1)
                    if kind < 2:
                        src = (w1s, w3s)[kind][0].rearrange("(k p) f -> p k f", p=P)[:, :, odd * P:(odd + 1) * P]
                    else:
                        src = w2s[0][odd * P:(odd + 1) * P, :]
                    sp.dma_start(ffn_half(0, 0, odd, kind)[2], src).then_inc(
                        raw_loaded[kind] if odd else first_loaded[kind], 16)
            sp.dma_start(cst[:, P:], consts[:, P:]).then_inc(consts_loaded, 16)
            for n in range(2):
                for kind in range(3 * n):
                    if n == 1:
                        u = MIX_UNITS - 3 + kind
                        sp.wait_ge(half_ready, MIX_HALF0 + 2 * u + 2)
                    ffn_load(sp, n, 0, kind)
                with sp.Fori(1, FI) as i:
                    for kind in range(3):
                        sp.wait_ge(half_ready, i * 6 + (FFN_HALF0[n] - 6 + 3 + kind + 1))
                        ffn_load(sp, n, i, kind)
                if n == 0:
                    for u in range(MIX_UNITS):
                        sp.wait_ge(half_ready, MIX_HALF0 - 3 + u + 1 if u < 3 else MIX_HALF0 + 2 * (u - 3) + 2)
                        mix_load(sp, u)
            for t in range(TT):
                for c in range(2):
                    sp.wait_ge(final_ready, 2 * t + c + 1)
                    cols = slice(c * 512, (c + 1) * 512)
                    sp.dma_start(out[t * P:(t + 1) * P, cols], normed[:, t, cols]).then_inc(out_stored, 16)
            sp.wait_ge(out_stored, 16 * 2 * TT)

        @block.gpsimd
        def _(pool):
            steps = [0]

            def step(ins):
                steps[0] += 1
                ins.then_inc(pool_step, 1)
                pool.wait_ge(pool_step, steps[0])

            step(pool.memset(minus_half[:, :], -0.5))

            def rsqrt(order, col, width):
                pool.wait_ge(sq_ready, order)
                m = mean_sq[:, col:col + 1]
                if width == D:
                    step(pool.tensor_scalar(m, sumsq[:, 0, col:col + 1], sumsq[:, 1, col:col + 1], EPS, ALU.add, ALU.add))
                else:
                    step(pool.tensor_scalar(m, sumsq[:, 0, col:col + 1], 1.0 / width, EPS, ALU.mult, ALU.add))
                pool.tensor_tensor(rstd[:, col:col + 1], m, minus_half[:, :], ALU.pow).then_inc(rstd_ready, 1)

            def rotate(tok):
                v = tok[:, :, :].rearrange("p t (h d) -> p t h d", h=HEADS)
                for t in range(TT):
                    r = v[:, t, :, 0:ROT]
                    sn = sin_t[:, t, :].unsqueeze(1).to_broadcast([P, HEADS, ROT])
                    cs = cos_t[:, t, :].unsqueeze(1).to_broadcast([P, HEADS, ROT])
                    hr = ROT // 2
                    pool.tensor_tensor(rot_t[:, t, :, 0:hr], r[:, :, hr:ROT], sn[:, :, 0:hr], ALU.mult)
                    step(pool.tensor_tensor(rot_t[:, t, :, hr:ROT], r[:, :, 0:hr], sn[:, :, hr:ROT], ALU.mult))
                    step(pool.tensor_tensor(r, r, cs, ALU.mult))
                    pool.tensor_tensor(r, r, rot_t[:, t, :, :], ALU.add).then_inc(rotated, 1)

            def softplus():
                v, e, w, p, dt = (dts[:, j, :, :] for j in (0, 2, 4, 5, 6))
                pool.wait_ge(atanh_arg, 1)
                step(pool.tensor_tensor(w, e, e, ALU.mult))
                step(pool.tensor_scalar(p, w, 1.0 / 15, None, ALU.mult))
                for k in (13, 11, 9, 7, 5, 3):
                    step(pool.tensor_scalar(p, p, 1.0 / k, None, ALU.add))
                    step(pool.tensor_tensor(p, p, w, ALU.mult))
                step(pool.tensor_scalar(p, p, 1.0, 2.0, ALU.add, ALU.mult))
                step(pool.tensor_tensor(p, p, e, ALU.mult))
                step(pool.tensor_scalar(v, v, 0.0, None, ALU.max))
                step(pool.tensor_tensor(dt, p, v, ALU.add))
                pool.wait_ge(neg_a_ready, 1)
                step(pool.tensor_scalar(w, dt, -1.0, None, ALU.mult))
                pool.tensor_tensor(w, w, dts[:, 3, 0, :].unsqueeze(1).to_broadcast([P, TT, SH]),
                                   ALU.mult).then_inc(a_ready, 1)

            for t in range(TT):
                rsqrt(2 * t + 2, t, D)
            pool.dma_start(wdt[:, :, :], w_in[:, D_IN - SH:D_IN].rearrange("(k p) f -> p k f", p=P)).then_inc(params_loaded, 16)
            pool.dma_start(conv_rows[0:TAPS * CT, :], conv_w.rearrange("k (c p) -> (k c) p", p=P)).then_inc(params_loaded, 16)
            pool.dma_start(conv_rows[TAPS * CT:, :], conv_b.rearrange("(c p) -> c p", p=P)).then_inc(params_loaded, 16)
            for j, v in enumerate((D_skip, A_log)):
                pool.dma_start(small[:, j, :], v.partition_broadcast(P)).then_inc(params_loaded, 16)
            pool.dma_start(bias_col[:, :], dt_bias.rearrange("(h a) -> h a", a=1)).then_inc(params_loaded, 16)
            pool.dma_start(norm_w[:, 1, :], norms[1].partition_broadcast(P)).then_inc(norm_loaded[1], 16)
            pool.dma_start(mix_w[:, 0:D_ATTN], attn_norm.partition_broadcast(P)).then_inc(mix_w_loaded, 16)
            pool.dma_start(mix_w[:, D_ATTN:], ssd_norm.partition_broadcast(P)).then_inc(mix_w_loaded, 16)
            pool.wait_ge(scaled, 4)
            pool.dma_start(norm_w[:, 0, :], norms[2].partition_broadcast(P)).then_inc(norm_loaded[2], 16)
            for t in range(TT):
                rsqrt(4 + 2 * t + 2, 2 + t, D)
            pool.wait_ge(scaled, 8)
            pool.dma_start(norm_w[:, 1, :], norms[3].partition_broadcast(P)).then_inc(norm_loaded[3], 16)
            softplus()
            pool.wait_ge(transposed, 8)
            for t in range(TT):
                for j in range(2):
                    pool.wait_ge(x_tok_ready, 2 * j + t + 1)
                    pool.tensor_tensor(
                        normed[:, t, D_ATTN + j * 512:D_ATTN + (j + 1) * 512].rearrange("p (h d) -> p h d", d=SP_),
                        x_tok[:, t, j * 512:(j + 1) * 512].rearrange("p (h d) -> p h d", d=SP_),
                        skip16[:, 8 * j:8 * j + 8].unsqueeze(2).to_broadcast([P, 8, SP_]), ALU.mult).then_inc(skip_ready, 1)
            pool.wait_ge(consts_loaded, 16)
            pool.wait_ge(proj_out, 4)
            rotate(q_tok)
            pool.wait_ge(proj_out, 6)
            rotate(k_tok)
            for t in range(TT):
                rsqrt(8 + t + 1, 4 + t, 512)
            for t in range(TT):
                rsqrt(10 + t + 1, 6 + t, 512)
            for t in range(TT):
                rsqrt(12 + t + 1, 8 + t, 512)
            for n in (2, 3):
                for t in range(TT):
                    rsqrt(14 + 4 * (n - 2) + 2 * t + 2, 2 * (n % 2) + t, D)

        @block.scalar
        def _(act):
            def split_hi(slot, src, loaded, count, columns):
                act.wait_ge(loaded, count)
                dst = w_hi[:, slot, :]
                act.activation(by_tile(dst) if columns else dst, src, ACT.Copy).then_inc(hi_ready, 1)

            def ffn_hi(n, i, odd, kind):
                _, slot, src = ffn_half(n, i, odd, kind)
                u0 = FFN_UNIT0[n] + kind
                split_hi(slot, src, raw_loaded[u0 % RAW_SLOTS], i * 16 + 16 * (u0 // RAW_SLOTS + 1), kind < 2)

            def first_hi(kind):
                _, slot, src = ffn_half(0, 0, 0, kind)
                split_hi(slot, src, first_loaded[kind], 16, kind < 2)

            def mix_hi(m):
                if HALF_SLOTS <= m < MIX_HALVES:
                    act.wait_ge(half_used, m - HALF_SLOTS + 1)
                _, slot, src = mix_half(m)
                u = MIX_UNIT0 + m // 2
                split_hi(slot, src, raw_loaded[u % RAW_SLOTS], 16 * (u // RAW_SLOTS + 1), by_columns(m))

            def square_x(n, t, c):
                if n:
                    act.wait_ge(x_ready, 4 * (n - 1) + 2 * t + c + 1)
                cols, r = slice(c * 512, (c + 1) * 512), 2 * (n % 2) + t
                act.activation(normed[:, t, cols], x[:, t, cols], ACT.Square, scale=D ** -0.5,
                               accum_out=sumsq[:, c, r:r + 1]).then_inc(sq_ready, 1)

            def hT_hi_part(count, bank_n, row, t):
                act.wait_ge(transposed, count)
                act.activation(hT_hi[:, row:row + 4, t * P:(t + 1) * P],
                               bank[:, bank_n, :].rearrange("p (k c) -> p k c", k=4), ACT.Copy).then_inc(hT_hi_ready, 1)

            def norm_hi(n, t):
                for j in range(2):
                    hT_hi_part(hT_count(n) + 2 * t + j + 1, T_BANKS[j], 4 * j, t)

            def gate(n, i, odd):
                f = FT * n + 2 * i + odd
                act.wait_ge(gate_done, f + 1)
                act.activation(silu_g, bank[:, G_BANK, 0:SEQ], ACT.Silu).then_inc(silu_ready, 1)
                act.wait_ge(gu_ready, f + 1)
                act.activation(gu_hi[:, odd, :], gu[:, :], ACT.Copy).then_inc(gu_hi_ready, 1)

            def ffn_step(n, i, odd):
                i2, odd2 = (i, 1) if not odd else (i + 1, 0)
                ffn_hi(n, i2, odd2, 0)
                ffn_hi(n, i2, odd2, 1)
                gate(n, i, odd)
                if not (isinstance(i, int) and i + odd == 0):
                    act.wait_ge(down_done, (FT - 1) * n + 2 * i + odd)
                ffn_hi(n, i2, odd2, 2)

            def ffn_steps(n):
                ffn_step(n, 0, 0)
                ffn_step(n, 0, 1)
                with act.Fori(1, FI - 1) as i:
                    ffn_step(n, i, 0)
                    ffn_step(n, i, 1)
                ffn_step(n, FI - 1, 0)

            for c in range(2):
                act.wait_ge(x_loaded[c], 16)
                square_x(0, 0, c)
            first_hi(0)
            norm_hi(0, 0)
            for c in range(2):
                act.wait_ge(x_loaded[2 + c], 16)
                square_x(0, 1, c)
            first_hi(1)
            norm_hi(0, 1)
            first_hi(2)

            ffn_steps(0)
            act.wait_ge(params_loaded, 16 * 6)
            act.activation(wdt_hi[:, :, :], wdt[:, :, :], ACT.Copy).then_inc(wdt_hi_ready, 1)
            act.wait_ge(consts_loaded, 16)
            act.activation(ident_r[:, :], ident, ACT.Copy).then_inc(consts_r, 1)
            act.activation(mask_r[:, :], cst[:, C_MASK:C_MASK + P], ACT.Copy).then_inc(consts_r, 1)
            act.wait_ge(conv_rows_T, 1)
            act.activation(conv_p[:, :, :], bank[:, 7, 0:(TAPS + 1) * CT].rearrange("p (k c) -> p k c", c=CT),
                           ACT.Copy).then_inc(conv_p_ready, 1)
            mix_hi(0)
            mix_hi(1)
            gate(0, FI - 1, 1)
            square_x(1, 0, 0)
            square_x(1, 0, 1)
            square_x(1, 1, 0)
            act.wait_ge(down_done, FT - 1)
            mix_hi(2)
            norm_hi(1, 0)
            square_x(1, 1, 1)
            mix_hi(3)
            norm_hi(1, 1)
            mix_hi(4)
            mix_hi(5)

            def chunk_out(c, t, func, dst):
                if c == "z0" and t == 0:
                    act.wait_ge(z0_first, 1)
                else:
                    act.wait_ge(half_used, M_CHUNK[c] + 4)
                act.activation(dst[:, t, :], bank[:, chunk_bank(c) + t, :], func).then_inc(proj_out, 1)

            def first_tap(j):
                act.wait_ge(half_used, M_CONV + j + 1)
                if j == 0:
                    act.wait_ge(conv_p_ready, 1)
                if j >= 4:
                    act.wait_ge(xbc_ready, j - 3)
                c = CONV_ORDER[j]
                act.activation(conv_acc[:, j % 4, :], bank[:, conv_bank(j), 0:SEQ], ACT.Identity,
                               bias=conv_p[:, TAPS, c:c + 1], scale=conv_p[:, TAPS - 1, c:c + 1]).then_inc(tap_ready, 1)

            def conv_silu(j):
                act.wait_ge(taps_done, j + 1)
                act.activation(xbc[:, CONV_ORDER[j], :], conv_acc[:, j % 4, :], ACT.Silu).then_inc(xbc_ready, 1)

            def x_tok_out(j):
                for t in range(TT):
                    act.wait_ge(xT_done, TT * j + t + 1)
                    act.activation(x_tok[:, t, j * 512:(j + 1) * 512], bank[:, 6 + t, :], ACT.Copy).then_inc(x_tok_ready, 1)

            def decay_exp(h):
                act.wait_ge(bc_done, h + 1)
                if h >= 2:
                    act.wait_ge(m_ready, 2 * (h - 1))
                for s, (a, b) in enumerate(((0, 256), (256, 384))):
                    act.activation(decay[:, h % 2, a:b], bank[:, 4 + h % 2, a:b], ACT.Exp,
                                   bias=dts[:, 7, s, h:h + 1]).then_inc(decay_ready, 1)

            def square_mix(col, first_col, count):
                for t in range(TT):
                    act.wait_ge(gated, count + t + 1)
                    act.activation(conv_acc[:, 2 * t:2 * t + 2, :],
                                   normed[:, t, first_col:first_col + 512].rearrange("p (a b) -> p a b", a=2), ACT.Square,
                                   accum_out=sumsq[:, 0, col + t:col + t + 1]).then_inc(sq_ready, 1)

            def qkT_out(dst, bank0, count):
                for t in range(TT):
                    act.wait_ge(qkT_done, count + t + 1)
                    act.activation(dst[:, :, t * P:(t + 1) * P], bank[:, bank0 + t, :].rearrange("p (k c) -> p k c", k=4),
                                   ACT.Copy).then_inc(qkT_ready, 1)

            def softmax_exp(h):
                act.wait_ge(max_ready, h + 1)
                if h >= 2:
                    act.wait_ge(probsT_done, h - 1)
                for t, (a, b) in enumerate(((0, 128), (128, 384))):
                    act.activation(probs[:, h % 2, a:b], bank[:, score_bank(h), a:b], ACT.Exp,
                                   bias=row_bias[:, h, t:t + 1], scale=HD ** -0.5,
                                   accum_out=row_sum[:, t, h:h + 1]).then_inc(probs_ready, 1)

            def probsT_out(h):
                act.wait_ge(probsT_done, h + 1)
                act.activation(probsT[:, h, :], bank[:, score_bank(h) + 1, 0:384], ACT.Copy).then_inc(probsT_ready, 1)

            for t in range(TT):
                chunk_out("z0", t, ACT.Silu, z_silu[:, :, 0:512])
                if t == 0:
                    for m in (6, 7, 8):
                        mix_hi(m)
            act.wait_ge(dtT_done, 1)
            act.activation(dtT[:, :], bank[0:SH, 7, 0:SEQ], ACT.Identity, bias=bias_col[:, :]).then_inc(dtT_ready, 1)
            for m in range(5, MIX_HALVES):
                if m < 17:
                    first_tap(m - 5)
                if m == 32:
                    for t in range(TT):
                        chunk_out("v", t, ACT.Copy, v_tok)
                if 30 <= m < 33:
                    probsT_out(2 * (m - 30))
                    probsT_out(2 * (m - 30) + 1)
                if m in (33, 34):
                    probsT_out(m - 27)
                if 29 <= m < 32:
                    softmax_exp(2 * (m - 29))
                    softmax_exp(2 * (m - 29) + 1)
                if m in (32, 33):
                    softmax_exp(m - 26)
                if m + 4 < MIX_HALVES:
                    mix_hi(m + 4)
                if m == 6:
                    act.wait_ge(dt_arg, 1)
                    act.activation(dts[:, 2, :, :], dts[:, 1, :, :], ACT.Exp).then_inc(dt_exp, 1)
                    act.activation(dts[:, 3, 0, :], alog16, ACT.Exp).then_inc(neg_a_ready, 1)
                if 7 <= m < 19:
                    conv_silu(m - 7)
                if m == 13:
                    for g in range(GROUPS):
                        act.wait_ge(cb_done, g + 1)
                        act.activation(cb[:, g, :], bank[:, 4 + g, 0:384], ACT.Copy).then_inc(cb_ready, 1)
                if m == 17:
                    x_tok_out(0)
                if m == 19:
                    x_tok_out(1)
                if m == 20:
                    for t in range(TT):
                        chunk_out("q", t, ACT.Copy, q_tok)
                if m == 24:
                    for t in range(TT):
                        chunk_out("k", t, ACT.Copy, k_tok)
                if 20 <= m < 28:
                    decay_exp(2 * (m - 20))
                    decay_exp(2 * (m - 20) + 1)
                if m == 23:
                    qkT_out(qT, 2, 0)
                if m == 25:
                    square_mix(4, D_ATTN, 0)
                if m == 27:
                    qkT_out(kT, 0, TT)
                if m == 28:
                    for t in range(TT):
                        hT_hi_part(8 + t + 1, 4 + t, 8, t)
                    for t in range(TT):
                        chunk_out("z1", t, ACT.Silu, z_silu[:, :, 512:1024])
                if m == 30:
                    square_mix(6, D_ATTN + 512, 2)
                if m == 35:
                    for t in range(TT):
                        hT_hi_part(10 + t + 1, 4 + t, 0, t)
                if m == 36:
                    square_mix(8, 0, 4)
                if m == 39:
                    for t in range(TT):
                        hT_hi_part(12 + t + 1, 4 + t, 4, t)
                if m == 40:
                    for kind in range(2):
                        act.wait_ge(half_used, 39 + kind)
                        ffn_hi(1, 0, 0, kind)
            square_x(2, 0, 0)
            square_x(2, 0, 1)
            norm_hi(2, 0)
            square_x(2, 1, 0)
            square_x(2, 1, 1)
            ffn_hi(1, 0, 0, 2)
            norm_hi(2, 1)

            ffn_steps(1)
            gate(1, FI - 1, 1)
            for t in range(TT):
                for c in range(2):
                    square_x(3, t, c)

        @block.vector
        def _(dve):
            steps = [0]

            def step(ins):
                steps[0] += 1
                ins.then_inc(dve_step, 1)
                dve.wait_ge(dve_step, steps[0])

            def split_lo(half, columns):
                h, slot, src = half
                dve.wait_ge(hi_ready, h + 1)
                hi, lo = w_hi[:, slot, :].bitcast(f32), w_lo[:, slot, :]
                if columns:
                    hi, lo = by_tile(hi), by_tile(lo)
                dve.tensor_tensor(lo, src, hi, ALU.subtract).then_inc(half_ready, 1)

            def ffn_lo(n, i, odd, kind):
                split_lo(ffn_half(n, i, odd, kind), kind < 2)

            def mix_lo(m):
                split_lo(mix_half(m), by_columns(m))

            def update_x(n, t, c):
                dve.wait_ge(acc_ready, 4 * (n - 1) + 2 * t + c + 1)
                xs = x[:, t, c * 512:(c + 1) * 512]
                dve.scalar_tensor_tensor(xs, bank[:, 2 * t + c, :], 1.0 if n == 2 else 0.5, xs,
                                         ALU.mult, ALU.add).then_inc(x_ready, 1)

            def scale_x(n, t):
                if t == 0:
                    dve.wait_ge(norm_loaded[n], 16)
                dve.wait_ge(rstd_ready, (0, 2, 10, 12)[n] + t + 1)
                r = 2 * (n % 2) + t
                for c in range(2):
                    cols = slice(c * 512, (c + 1) * 512)
                    dve.scalar_tensor_tensor(normed[:, t, cols], x[:, t, cols], rstd[:, r:r + 1], norm_w[:, n % 2, cols],
                                             ALU.mult, ALU.mult).then_inc(final_ready if n == 3 else scaled, 1)

            def hT_lo_part(count, bank_n, row, t):
                dve.wait_ge(hT_hi_ready, count)
                part = slice(t * P, (t + 1) * P)
                dve.tensor_tensor(hT_lo[:, row:row + 4, part],
                                  bank[:, bank_n, :].rearrange("p (k c) -> p k c", k=4),
                                  hT_hi[:, row:row + 4, part].bitcast(f32), ALU.subtract).then_inc(hT_ready, 1)

            def norm_lo(n, t):
                for j in range(2):
                    hT_lo_part(hT_count(n) + 2 * t + j + 1, T_BANKS[j], 4 * j, t)

            def up(n, i, odd):
                f = FT * n + 2 * i + odd
                dve.wait_ge(up_done, f + 1)
                dve.wait_ge(silu_ready, f + 1)
                if not (isinstance(f, int) and f == 0):
                    dve.wait_ge(gu_split, f)
                dve.tensor_tensor(gu[:, :], bank[:, U_BANK, 0:SEQ], silu_g, ALU.mult).then_inc(gu_ready, 1)
                dve.wait_ge(gu_hi_ready, f + 1)
                dve.tensor_tensor(gu_lo[:, odd, :], gu[:, :], gu_hi[:, odd, :].bitcast(f32),
                                  ALU.subtract).then_inc(gu_split, 1)

            def ffn_step(n, i, odd):
                i2, odd2 = (i, 1) if not odd else (i + 1, 0)
                ffn_lo(n, i2, odd2, 0)
                ffn_lo(n, i2, odd2, 1)
                up(n, i, odd)
                ffn_lo(n, i2, odd2, 2)

            def ffn_steps(n):
                ffn_step(n, 0, 0)
                ffn_step(n, 0, 1)
                with dve.Fori(1, FI - 1) as i:
                    ffn_step(n, i, 0)
                    ffn_step(n, i, 1)
                ffn_step(n, FI - 1, 0)

            for c in range(2):
                dve.wait_ge(x_loaded[c], 16)
            scale_x(0, 0)
            ffn_lo(0, 0, 0, 0)
            norm_lo(0, 0)
            for c in range(2):
                dve.wait_ge(x_loaded[2 + c], 16)
            scale_x(0, 1)
            ffn_lo(0, 0, 0, 1)
            norm_lo(0, 1)
            ffn_lo(0, 0, 0, 2)

            ffn_steps(0)
            dve.wait_ge(wdt_hi_ready, 1)
            dve.tensor_tensor(wdt_lo[:, :, :], wdt[:, :, :], wdt_hi[:, :, :].bitcast(f32),
                              ALU.subtract).then_inc(wdt_ready, 1)
            mix_lo(0)
            mix_lo(1)
            up(0, FI - 1, 1)
            update_x(1, 0, 0)
            update_x(1, 0, 1)
            update_x(1, 1, 0)
            scale_x(1, 0)
            update_x(1, 1, 1)
            mix_lo(2)
            norm_lo(1, 0)
            scale_x(1, 1)
            mix_lo(3)
            norm_lo(1, 1)
            mix_lo(4)
            mix_lo(5)

            v, cs, ncs = (dts[:, j, :, :] for j in (0, 1, 7))

            def softplus_argument():
                dve.wait_ge(dt_done, 1)
                step(dve.tensor_copy(v, bank[:, 6, 0:TT * SH].rearrange("p (t h) -> p t h", t=TT)))
                dve.scalar_tensor_tensor(dts[:, 1, :, :], v, -1.0, v, ALU.mult, ALU.min).then_inc(dt_arg, 1)

            def atanh_argument():
                e, w, p = (dts[:, j, :, :] for j in (2, 4, 5))
                dve.wait_ge(dt_exp, 1)
                step(dve.tensor_scalar(w, e, 2.0, None, ALU.add))
                step(dve.reciprocal(p, w))
                dve.tensor_tensor(e, e, p, ALU.mult).then_inc(atanh_arg, 1)

            def cumsum_out():
                dve.wait_ge(cs_done, 1)
                dve.tensor_copy(cs, bank[:, 6, 0:TT * SH].rearrange("p (t h) -> p t h", t=TT)).then_inc(cs_tok_ready, 1)
                dve.wait_ge(cs_tok_ready, 1)
                step(dve.tensor_scalar(ncs, cs, -1.0, None, ALU.mult))

            def cumsum_T_out():
                dve.wait_ge(csT_done, 1)
                step(dve.tensor_copy(csT_hi[:, :], bank[0:SH, 7, 0:SEQ]))
                dve.tensor_tensor(csT_lo[:, :], bank[0:SH, 7, 0:SEQ], csT_hi[:, :].bitcast(f32),
                                  ALU.subtract).then_inc(csT_ready, 1)

            def conv_taps(j0):
                dve.wait_ge(tap_ready, j0 + 2)
                done = {}
                for s in (1, 2, 3):
                    for j in (j0, j0 + 1):
                        acc, u, c = conv_acc[:, j % 4, :], bank[:, conv_bank(j), :], CONV_ORDER[j]
                        if s > 1:
                            dve.wait_ge(dve_step, done[j])
                        ins = dve.scalar_tensor_tensor(acc[:, s:SEQ], u[:, 0:SEQ - s],
                                                       conv_p[:, TAPS - 1 - s, c:c + 1], acc[:, s:SEQ],
                                                       ALU.mult, ALU.add)
                        if s < 3:
                            steps[0] += 1
                            ins.then_inc(dve_step, 1)
                            done[j] = steps[0]
                        else:
                            ins.then_inc(taps_done, 1)

            def weigh(h):
                g = h // 8
                if h == 0:
                    dve.wait_ge(cb_ready, 2)
                if h >= 2:
                    dve.wait_ge(y_done, h - 1)
                for s, (a, b) in enumerate(((0, 256), (256, 384))):
                    dve.wait_ge(decay_ready, 2 * h + s + 1)
                    dve.scalar_tensor_tensor(mix_m[:, h % 2, a:b], cb[:, g, a:b], dts[:, 6, s, h:h + 1],
                                             decay[:, h % 2, a:b], ALU.mult, ALU.mult).then_inc(m_ready, 1)

            def ssd_add(g):
                cols = slice(D_ATTN + 512 * g, D_ATTN + 512 * (g + 1))
                dve.wait_ge(y_done, 8 * (g + 1))
                dve.wait_ge(skip_ready, 4)
                for t in range(TT):
                    dve.tensor_tensor(normed[:, t, cols], bank[:, 6 + t, :], normed[:, t, cols], ALU.add).then_inc(y_added, 1)

            def ssd_gate(g):
                cols = slice(D_ATTN + 512 * g, D_ATTN + 512 * (g + 1))
                for t in range(TT):
                    dve.wait_ge(y_added, 2 * g + t + 1)
                    dve.wait_ge(proj_out, 8 if g else 2)
                    dve.tensor_tensor(normed[:, t, cols], normed[:, t, cols], z_silu[:, t, 512 * g:512 * (g + 1)],
                                      ALU.mult).then_inc(gated, 1)

            def mix_scale(col, cols, count):
                dve.wait_ge(mix_w_loaded, 32)
                for t in range(TT):
                    dve.wait_ge(rstd_ready, count + t + 1)
                    dve.scalar_tensor_tensor(normed[:, t, cols], normed[:, t, cols], rstd[:, col + t:col + t + 1],
                                             mix_w[:, cols], ALU.mult, ALU.mult).then_inc(scaled, 1)

            def score_max(h):
                dve.wait_ge(scores_done, h + 1)
                dve.reduce_max(row_max[:, h, 0:1], bank[:, score_bank(h), 0:128], axis=AX.X)
                step(dve.reduce_max(row_max[:, h, 1:2], bank[:, score_bank(h), 128:384], axis=AX.X))
                dve.tensor_scalar(row_bias[:, h, :], row_max[:, h, :], -(HD ** -0.5), None, ALU.mult).then_inc(max_ready, 1)

            def attention_out():
                dve.wait_ge(probs_ready, 2 * HEADS)
                step(dve.reciprocal(row_inv[:, :, :], row_sum[:, :, :]))
                dve.wait_ge(pv_done, HEADS)
                for t in range(TT):
                    dve.tensor_tensor(normed[:, t, 0:D_ATTN].rearrange("p (h d) -> p h d", d=HD),
                                      bank[:, 6 + t, :].rearrange("p (h d) -> p h d", d=HD),
                                      row_inv[:, t, :].unsqueeze(2).to_broadcast([P, HEADS, HD]), ALU.mult).then_inc(gated, 1)

            for m in (6, 7, 8):
                mix_lo(m)
            softplus_argument()
            for m in range(5, MIX_HALVES):
                if m in (24, 28):
                    ssd_add(m // 4 - 6)
                if 29 <= m < 32:
                    score_max(2 * (m - 29))
                    score_max(2 * (m - 29) + 1)
                if m in (32, 33):
                    score_max(m - 26)
                if m + 4 < MIX_HALVES:
                    mix_lo(m + 4)
                if m < 18 and m % 2 == 0:
                    conv_taps(m - 6)
                if m == 7:
                    atanh_argument()
                if m == 13:
                    cumsum_out()
                if m == 15:
                    cumsum_T_out()
                if 20 <= m < 28:
                    weigh(2 * (m - 20))
                    weigh(2 * (m - 20) + 1)
                if m == 24:
                    ssd_gate(0)
                if m == 26:
                    mix_scale(4, slice(D_ATTN, D_ATTN + 512), 4)
                if m == 28:
                    for t in range(TT):
                        hT_lo_part(8 + t + 1, 4 + t, 8, t)
                if m == 29:
                    ssd_gate(1)
                if m == 32:
                    mix_scale(6, slice(D_ATTN + 512, D_MIX), 6)
                if m == 35:
                    for t in range(TT):
                        hT_lo_part(10 + t + 1, 4 + t, 0, t)
                    attention_out()
                if m == 37:
                    mix_scale(8, slice(0, D_ATTN), 8)
                if m == 39:
                    for t in range(TT):
                        hT_lo_part(12 + t + 1, 4 + t, 4, t)
                if m == 40:
                    for kind in range(2):
                        ffn_lo(1, 0, 0, kind)
            update_x(2, 0, 0)
            update_x(2, 0, 1)
            scale_x(2, 0)
            update_x(2, 1, 0)
            norm_lo(2, 0)
            update_x(2, 1, 1)
            scale_x(2, 1)
            ffn_lo(1, 0, 0, 2)
            norm_lo(2, 1)

            ffn_steps(1)
            up(1, FI - 1, 1)
            update_x(3, 0, 0)
            update_x(3, 0, 1)
            update_x(3, 1, 0)
            scale_x(3, 0)
            update_x(3, 1, 1)
            scale_x(3, 1)

        @block.tensor
        def _(pe):
            def three(dst, lhs, rhs, start, stop):
                pe.matmul(dst, lhs[0], rhs[0], start=start, stop=False, skip_group_check=True)
                pe.matmul(dst, lhs[0], rhs[1], start=False, stop=False, skip_group_check=True)
                return pe.matmul(dst, lhs[1], rhs[0], start=False, stop=stop, skip_group_check=True)

            def hT(k, part):
                return hT_hi[:, k, part], hT_lo[:, k, part]

            def w_cols(slot, k):
                return tuple(w[:, slot, k * P:(k + 1) * P] for w in (w_hi, w_lo))

            def tok(t):
                return slice(t * P, (t + 1) * P)

            def columns_product(slot, dst, part=slice(0, SEQ)):
                for k in range(KD):
                    last = three(dst[:, part], w_cols(slot, k), hT(k, part), k == 0, k == KD - 1)
                return last

            def down(n, i, odd, t, c, start, stop):
                slot = ffn_half(n, i, odd, 2)[1]
                return three(bank[:, 2 * t + c, :], (gu_hi[:, odd, tok(t)], gu_lo[:, odd, tok(t)]),
                             tuple(w[:, slot, c * 512:(c + 1) * 512] for w in (w_hi, w_lo)), start, stop)

            def down_both(n, i, odd, start):
                for t in range(TT):
                    for c in range(2):
                        last = down(n, i, odd, t, c, start, False)
                last.then_inc(down_done, 1)

            def down_waits(n, i, odd):
                pe.wait_ge(half_ready, ffn_half(n, i, odd, 2)[0] + 1)
                pe.wait_ge(gu_split, FT * n + 2 * i + odd + 1)

            def gate_up(n, i, odd):
                f = FT * n + 2 * i + odd
                for kind, dst, done, free in ((0, G_BANK, gate_done, silu_ready), (1, U_BANK, up_done, gu_ready)):
                    h, slot, _ = ffn_half(n, i, odd, kind)
                    pe.wait_ge(half_ready, h + 1)
                    if not (isinstance(f, int) and f == 0):
                        pe.wait_ge(free, f)
                    columns_product(slot, bank[:, dst, :]).then_inc(done, 1)

            def keep_clock(count):
                for _ in range(count):
                    pe.matmul(bank[:, U_BANK, 0:P], ident, ident, start=True, stop=True)

            def ffn(n):
                norm_transposes(2 * n, 0)
                keep_clock(5)
                for t in range(TT):
                    pe.wait_ge(hT_ready, hT_count(2 * n) + 2 * t + 2)
                    for kind, dst, done in ((0, G_BANK, gate_done), (1, U_BANK, up_done)):
                        if t == 0 and kind == 1:
                            norm_transposes(2 * n, 1)
                        h, slot, _ = ffn_half(n, 0, 0, kind)
                        if t == 0:
                            pe.wait_ge(half_ready, h + 1)
                        last = columns_product(slot, bank[:, dst, :], tok(t))
                        if t == TT - 1:
                            last.then_inc(done, 1)
                gate_up(n, 0, 1)
                down_waits(n, 0, 0)
                down_both(n, 0, 0, True)
                with pe.Fori(1, FI - 1) as i:
                    gate_up(n, i, 0)
                    down_waits(n, i - 1, 1)
                    down_both(n, i - 1, 1, False)
                    gate_up(n, i, 1)
                    down_waits(n, i, 0)
                    down_both(n, i, 0, False)
                i = FI - 1
                if n == 0:
                    pe.wait_ge(consts_loaded, 16)
                    pe.wait_ge(params_loaded, 16 * 6)
                    pe.transpose(bank[:, 7, 0:(TAPS + 1) * CT], conv_rows[:, :],
                                 cst[0:(TAPS + 1) * CT, C_ID:C_ID + (TAPS + 1) * CT]).then_inc(conv_rows_T, 1)
                gate_up(n, i, 0)
                down_waits(n, i - 1, 1)
                down_both(n, i - 1, 1, False)
                gate_up(n, i, 1)
                down_waits(n, i, 0)
                for c in range(2):
                    down(n, i, 0, 0, c, False, False)
                down_waits(n, i, 1)
                for c in range(2):
                    down(n, i, 1, 0, c, False, True).then_inc(acc_ready, 1)
                for c in range(2):
                    last = down(n, i, 0, 1, c, False, False)
                    if c:
                        last.then_inc(down_done, 1)
                    down(n, i, 1, 1, c, False, True).then_inc(acc_ready, 1)

            def transpose_rows(t, col, bank_n):
                for k in range(4):
                    last = pe.transpose(bank[:, bank_n, k * P:(k + 1) * P],
                                        normed[:, t, col + k * P:col + (k + 1) * P], ident)
                last.then_inc(transposed, 1)

            def norm_transposes(n, t):
                for j in range(2):
                    pe.wait_ge(scaled, (0, 4, 14)[n] + 2 * t + j + 1)
                    if t:
                        pe.wait_ge(hT_ready, hT_count(n) + j + 1)
                    transpose_rows(t, 512 * j, T_BANKS[j])

            pe.wait_ge(ident_loaded, 16)
            keep_clock(4)
            ffn(0)

            def dt_product():
                pe.wait_ge(wdt_ready, 1)
                for k in range(KD):
                    last = three(bank[0:SH, 7, 0:SEQ], (wdt_hi[:, k, :], wdt_lo[:, k, :]), hT(k, slice(0, SEQ)),
                                 k == 0, k == KD - 1)
                last.then_inc(dtT_done, 1)

            def dt_transposes():
                pe.wait_ge(dtT_ready, 1)
                for t in range(TT):
                    last = pe.transpose(bank[:, 6, t * SH:(t + 1) * SH], dtT[:, tok(t)], ident[0:SH, 0:SH])
                last.then_inc(dt_done, 1)

            def conv_half(j):
                pe.wait_ge(half_ready, MIX_HALF0 + M_CONV + j + 1)
                if j >= 4:
                    pe.wait_ge(taps_done, j - 3)
                if j in (2, 3):
                    pe.wait_ge(proj_out, j - 1)
                columns_product(mix_half(M_CONV + j)[1], bank[:, conv_bank(j), :]).then_inc(half_used, 1)

            def cumsum():
                pe.wait_ge(a_ready, 1)
                a = dts[:, 4, :, :]
                pe.matmul(bank[:, 6, 0:SH], tri[:, 0:P], a[:, 0, :], start=True, stop=True)
                pe.matmul(bank[:, 6, SH:2 * SH], tri[:, P:SEQ], a[:, 0, :], start=True, stop=False)
                pe.matmul(bank[:, 6, SH:2 * SH], tri[:, 0:P], a[:, 1, :], start=False, stop=True).then_inc(cs_done, 1)

            def cumsum_T():
                pe.wait_ge(cs_tok_ready, 1)
                for t in range(TT):
                    last = pe.transpose(bank[0:SH, 7, tok(t)], dts[:, 1, t, :], ident)
                last.then_inc(csT_done, 1)

            def cb_products():
                pe.wait_ge(xbc_ready, 4)
                for g in range(GROUPS):
                    b, c = xbc[:, 8 + g, :], xbc[:, 10 + g, :]
                    pe.matmul(bank[:, 4 + g, 0:SEQ], b[:, 0:P], c, start=True, stop=True)
                    pe.matmul(bank[:, 4 + g, SEQ:SEQ + P], b[:, P:SEQ], c[:, P:SEQ], start=True, stop=True).then_inc(cb_done, 1)

            def x_transposes(j):
                pe.wait_ge(xbc_ready, 4 + 4 * (j + 1))
                if j == 1:
                    pe.wait_ge(x_tok_ready, 2)
                else:
                    pe.wait_ge(csT_ready, 1)
                for t in range(TT):
                    for k in range(4):
                        last = pe.transpose(bank[:, 6 + t, k * P:(k + 1) * P], xbc[:, 4 * j + k, tok(t)], ident)
                    last.then_inc(xT_done, 1)

            def chunk_part(m, t):
                b, q, slot = chunk_bank(chunk_of(m)), m % 4, mix_half(m)[1]
                for k in range(2):
                    last = three(bank[:, b + t, :], hT(2 * q + k, tok(t)),
                                 tuple(w[:, slot, k * 512:(k + 1) * 512] for w in (w_hi, w_lo)),
                                 q == 0 and k == 0, q == 3 and k == 1)
                return last

            def first_chunk():
                norm_transposes(1, 0)
                keep_clock(5)
                for t in range(TT):
                    pe.wait_ge(hT_ready, 4 + 2 * t + 2)
                    for m in range(4):
                        if t == 0 and m == 2:
                            norm_transposes(1, 1)
                        if t == 0:
                            pe.wait_ge(half_ready, MIX_HALF0 + m + 1)
                        last = chunk_part(m, t)
                        if t == 1:
                            last.then_inc(half_used, 1)
                        elif m == 3:
                            last.then_inc(z0_first, 1)

            def chunk_half(m):
                pe.wait_ge(half_ready, MIX_HALF0 + m + 1)
                if m == M_CHUNK["q"]:
                    pe.wait_ge(taps_done, 10)
                if m == M_CHUNK["k"]:
                    pe.wait_ge(taps_done, 12)
                if m == M_CHUNK["z1"]:
                    pe.wait_ge(qkT_ready, 2)
                if m == M_CHUNK["v"]:
                    pe.wait_ge(qkT_ready, 4)
                chunk_part(m, 0)
                chunk_part(m, 1).then_inc(half_used, 1)

            def decay_args(h):
                b = bank[:, 4 + h % 2, :]
                if h >= 2:
                    pe.wait_ge(decay_ready, 2 * (h - 1))
                else:
                    pe.wait_ge(cb_ready, 2)
                    pe.wait_ge(csT_ready, 1)
                    pe.wait_ge(consts_r, 2)
                head = ident_r[0:SH, h:h + 1].to_broadcast([SH, P])
                first = True
                for a, c, lo in ((0, SEQ, 0), (SEQ, SEQ + P, P)):
                    for part in (csT_hi, csT_lo):
                        pe.matmul(b[:, a:c], head, part[:, lo:SEQ], start=first, stop=False, skip_group_check=True)
                        first = False
                for a in (0, SEQ):
                    last = pe.matmul(b[:, a:a + P], ident_r[:, :], mask_r[:, :], start=False, stop=a > 0,
                                     skip_group_check=True)
                last.then_inc(bc_done, 1)

            def ssd_out(h):
                pe.wait_ge(m_ready, 2 * (h + 1))
                if h == 0:
                    pe.wait_ge(x_tok_ready, 4)
                if h == 8:
                    pe.wait_ge(y_added, 2)
                m, c, o = mix_m[:, h % 2, :], slice(h * SP_, (h + 1) * SP_), slice((h % 8) * SP_, (h % 8 + 1) * SP_)
                pe.matmul(bank[:, 6, o], m[:, 0:P], x_tok[:, 0, c], start=True, stop=True)
                pe.matmul(bank[:, 7, o], m[:, P:SEQ], x_tok[:, 0, c], start=True, stop=False)
                pe.matmul(bank[:, 7, o], m[:, SEQ:SEQ + P], x_tok[:, 1, c], start=False, stop=True).then_inc(y_done, 1)

            def mix_transposes(count, col, free, free_count):
                pe.wait_ge(free, free_count)
                for t in range(TT):
                    pe.wait_ge(scaled, count + t + 1)
                    transpose_rows(t, col, 4 + t)

            def qk_transposes(tensor, bank0, count):
                pe.wait_ge(rotated, count)
                for t in range(TT):
                    for k in range(4):
                        last = pe.transpose(bank[:, bank0 + t, k * P:(k + 1) * P], tensor[:, t, k * P:(k + 1) * P], ident)
                    last.then_inc(qkT_done, 1)

            def scores(h):
                r, p, b = slice(HD * (h % 2), HD * (h % 2 + 1)), h // 2, bank[:, score_bank(h), :]
                if h == 0:
                    pe.wait_ge(qkT_ready, 4)
                    pe.wait_ge(hT_ready, 10)
                if h == 1:
                    pe.wait_ge(proj_out, 8)
                if h >= 2:
                    pe.wait_ge(probs_ready, 2 * (h - 1) if h < 7 else 2 * h)
                pe.matmul(b[:, 0:P], qT[r, p, 0:P], kT[r, p, 0:P], start=True, stop=False, skip_group_check=True)
                pe.matmul(b[:, P:P + SEQ], qT[r, p, P:SEQ], kT[r, p, :], start=False, stop=False, skip_group_check=True)
                for a in (0, SEQ):
                    last = pe.matmul(b[:, a:a + P], mask_r[:, :], ident_r[:, :], start=False, stop=a > 0,
                                     skip_group_check=True)
                last.then_inc(scores_done, 1)

            def probs_transposes(h):
                pe.wait_ge(probs_ready, 2 * (h + 1))
                if h >= 2:
                    pe.wait_ge(probsT_ready, h - 1 if h < 7 else h)
                for a in range(3):
                    last = pe.transpose(bank[:, score_bank(h) + 1, a * P:(a + 1) * P],
                                        probs[:, h % 2, a * P:(a + 1) * P], ident)
                last.then_inc(probsT_done, 1)

            def pv(h):
                pe.wait_ge(probsT_ready, h + 1)
                if h == 0:
                    pe.wait_ge(proj_out, 10)
                    pe.wait_ge(y_added, 4)
                pt, c = probsT[:, h, :], slice(h * HD, (h + 1) * HD)
                pe.matmul(bank[:, 6, c], pt[:, 0:P], v_tok[:, 0, c], start=True, stop=True)
                pe.matmul(bank[:, 7, c], pt[:, P:SEQ], v_tok[:, 0, c], start=True, stop=False)
                pe.matmul(bank[:, 7, c], pt[:, SEQ:SEQ + P], v_tok[:, 1, c], start=False, stop=True).then_inc(pv_done, 1)

            def out_part(j, t, c):
                slot = mix_half(M_OUT + j)[1]
                return three(bank[:, 2 * t + c, :], hT(mix_row(OUT_ROWS[j]), tok(t)),
                             tuple(w[:, slot, c * 512:(c + 1) * 512] for w in (w_hi, w_lo)), j == 0, j == 11)

            def out_half(j):
                pe.wait_ge(half_ready, MIX_HALF0 + M_OUT + j + 1)
                if j == 0:
                    pe.wait_ge(proj_out, 10)
                    pe.wait_ge(hT_ready, 10)
                if j == 4:
                    pe.wait_ge(hT_ready, 12)
                for t in range(TT):
                    if j == 0 and t == 1:
                        pe.wait_ge(probsT_ready, 6)
                    for c in range(2):
                        last = out_part(j, t, c)
                last.then_inc(half_used, 1)

            def out_attention():
                pe.wait_ge(hT_ready, 14)
                for t in range(TT):
                    for c in range(2):
                        for j in range(8, 12):
                            if t == 0 and c == 0:
                                pe.wait_ge(half_ready, MIX_HALF0 + M_OUT + j + 1)
                            last = out_part(j, t, c)
                        last.then_inc(acc_ready, 1)

            first_chunk()
            dt_product()
            for m in range(M_CONV, M_OUT + 8):
                if m < M_CONV + CT:
                    conv_half(m - M_CONV)
                elif m < M_OUT:
                    chunk_half(m)
                else:
                    out_half(m - M_OUT)
                if m == 4:
                    dt_transposes()
                if m == 12:
                    cumsum()
                    cb_products()
                if m == 14:
                    cumsum_T()
                if m == 16:
                    x_transposes(0)
                if m == 18:
                    x_transposes(1)
                if m == 19:
                    decay_args(0)
                    decay_args(1)
                if 20 <= m < 28:
                    for h in (2 * (m - 20), 2 * (m - 20) + 1):
                        ssd_out(h)
                        if h + 2 < SH:
                            decay_args(h + 2)
                if m == 22:
                    qk_transposes(q_tok, 2, 2)
                if m == 26:
                    qk_transposes(k_tok, 0, 4)
                if m == 27:
                    mix_transposes(8, D_ATTN, decay_ready, 2 * SH)
                if 29 <= m < 32:
                    probs_transposes(2 * (m - 29))
                    probs_transposes(2 * (m - 29) + 1)
                if 28 <= m < 31:
                    scores(2 * (m - 28))
                    scores(2 * (m - 28) + 1)
                if m == 32:
                    probs_transposes(6)
                if m in (31, 32):
                    scores(m - 25)
                if m == 32:
                    for h in range(4):
                        pv(h)
                if m == 33:
                    probs_transposes(7)
                    pv(4)
                    pv(5)
                if m == 34:
                    pv(6)
                    pv(7)
                    mix_transposes(10, D_ATTN + 512, probsT_ready, HEADS)
                if m == 38:
                    mix_transposes(12, 0, hT_ready, 12)
            out_attention()
            ffn(1)


def by_columns(m):
    return M_CONV <= m < M_CONV + CT


def chunk_of(m):
    return next(c for c in CHUNKS if M_CHUNK[c] <= m < M_CHUNK[c] + 4)


def hT_count(n):
    return (0, 4, 14)[n]


def chunk_bank(c):
    return {"z0": 0, "q": 2, "k": 0, "z1": 2, "v": 0}[c]


def conv_bank(j):
    return (j + 2) % 4


def score_bank(h):
    return 2 if h in (1, 3, 5) else 4


_INS = ["x", "ffn1_norm", "ffn1_w1", "ffn1_w3", "ffn1_w2", "mix_norm", "w_in", "conv_w", "conv_b",
        "dt_bias", "A_log", "D_skip", "attn_out_norm", "ssd_out_norm", "w_out",
        "ffn2_norm", "ffn2_w1", "ffn2_w3", "ffn2_w2", "final_norm"]


def kernel(**inputs):
    import concourse.bacc as bacc
    from concourse.bass_utils import run_bass_kernel_spmd

    nc = bacc.Bacc("TRN2", target_bir_lowering=False, num_devices=1)
    arrays, t = {}, {}
    for name in _INS + ["shape_constants"]:
        if name == "shape_constants":
            a = shape_constants()
        else:
            a = np.ascontiguousarray(inputs[name])
            if name != "final_norm":
                a = a[0]
        arrays[f"in_{name}"] = a
        t[name] = nc.dram_tensor(f"in_{name}", a.shape, mybir.dt.from_np(a.dtype), kind="ExternalInput").ap()
    out = nc.dram_tensor("out_x", (SEQ, D), mybir.dt.float32, kind="ExternalOutput").ap()
    build(nc, t["x"], (t["ffn1_w1"], t["ffn2_w1"]), (t["ffn1_w3"], t["ffn2_w3"]), (t["ffn1_w2"], t["ffn2_w2"]),
          (t["ffn1_norm"], t["mix_norm"], t["ffn2_norm"], t["final_norm"]), t["w_in"], t["conv_w"], t["conv_b"],
          t["dt_bias"], t["A_log"], t["D_skip"], t["attn_out_norm"], t["ssd_out_norm"], t["w_out"],
          t["shape_constants"], out)
    r = run_bass_kernel_spmd(nc, [arrays], core_ids=[0])
    return r.results[0]["out_x"].reshape(1, SEQ, D)
```

```python
from contextlib import ExitStack

import numpy as np
import concourse.bass as bass
from concourse import mybir

P = 128
SEQ, D, F = 256, 1024, 2816
TT = SEQ // P
KD = D // P
HEADS, HD, ROT = 8, 64, 16
D_ATTN = HEADS * HD
SH, SP_, GROUPS = 16, 64, 2
D_SSM = SH * SP_
N_STATE, TAPS = 128, 4
D_CONV = D_SSM + 2 * GROUPS * N_STATE
D_IN = 3 * D_ATTN + D_SSM + D_CONV + SH
D_MIX = D_ATTN + D_SSM
CT = D_CONV // P
EPS = 1e-6
THETA = 500000.0
MASKED = -(2.0 ** 99)

RAW_SLOTS, HALF_SLOTS = 3, 6
HALF = 1024
FT = F // P
PAIR_ORDER = ((0, 0), (0, 1), (1, 0), (1, 1), (0, 2), (1, 2))
FI = FT // 2

MIX_UNIT0 = 3 * FI
CONV_ORDER = (8, 9, 10, 11, 0, 1, 2, 3, 4, 5, 6, 7)
CHUNKS = ("z0", "q", "k", "z1", "v")
M_CHUNK = {"z0": 0, "q": 16, "k": 20, "z1": 24, "v": 28}
M_CONV, M_OUT = 4, 32
CHUNK_COL = {"q": 0, "k": D_ATTN, "v": 2 * D_ATTN, "z0": 3 * D_ATTN, "z1": 3 * D_ATTN + 512}
OUT_ROWS = (4, 5, 6, 7, 8, 9, 10, 11, 0, 1, 2, 3)
MIX_HALVES = 12 + 4 * len(CHUNKS) + 12
MIX_UNITS = MIX_HALVES // 2
MIX_HALF0 = 6 * FI
FFN_UNIT0 = (0, MIX_UNIT0 + MIX_UNITS)
FFN_HALF0 = (0, MIX_HALF0 + MIX_HALVES)

C_ID, C_TRI, C_MASK, C_COS, C_SIN, C_SEL, C_END = 0, 128, 384, 512, 544, 576, 592
CS_ROWS = 3 * SH

def mix_row(r):
    return {0: 4, 1: 8, 2: 0}[r // 4] + r % 4


def shape_constants():
    c = np.zeros((P, C_END), np.float32)
    c[:, C_ID:C_ID + P] = np.eye(P)
    c[:, C_TRI:C_TRI + P] = np.triu(np.ones((P, P)))
    c[:, C_TRI + P:C_TRI + 2 * P] = 1.0
    c[:, C_MASK:C_MASK + P] = np.where(np.triu(np.ones((P, P))) > 0, 0.0, MASKED)
    inv = (np.float32(THETA) ** (-np.arange(0, ROT, 2, dtype=np.float32) / np.float32(ROT))).astype(np.float32)
    ang = np.arange(SEQ, dtype=np.float32)[:, None] * inv[None, :]
    cos, sin = (f(ang).astype(np.float32).reshape(TT, P, ROT // 2).transpose(1, 0, 2) for f in (np.cos, np.sin))
    c[:, C_COS:C_COS + TT * ROT] = np.concatenate([cos, cos], -1).reshape(P, -1)
    c[:, C_SIN:C_SIN + TT * ROT] = np.concatenate([-sin, sin], -1).reshape(P, -1)
    for r in range(SH):
        c[[r, 2 * SH + r], C_SEL + r] = 1.0
    return c


def build(nc, x_in, w1s, w3s, w2s, norms, w_in, conv_w, conv_b, dt_bias, A_log, D_skip,
          attn_norm, ssd_norm, w_out, consts, out):
    f32, f32r = mybir.dt.float32, mybir.dt.float32r
    ALU, ACT, AX = mybir.AluOpType, mybir.ActivationFunctionType, mybir.AxisListType

    with ExitStack() as ctx:
        def sb(name, shape, dtype=f32):
            return ctx.enter_context(nc.sbuf_tensor(name, shape, dtype))

        def sem(name):
            return ctx.enter_context(nc.semaphore(name))

        raw = sb("raw", [P, RAW_SLOTS, 2 * HALF])
        w_hi = sb("w_hi", [P, HALF_SLOTS, HALF], f32r)
        w_lo = sb("w_lo", [P, HALF_SLOTS, HALF], f32r)
        x = sb("x", [P, TT, D])
        hT_hi = sb("hT_hi", [P, 12, SEQ], f32r)
        hT_lo = sb("hT_lo", [P, 12, SEQ], f32r)
        normed = sb("normed", [P, TT, D_MIX])
        norm_w = sb("norm_w", [P, 2, D])
        mix_w = sb("mix_w", [P, D_MIX])
        cst = sb("cst", [P, C_END])
        ident_r = sb("ident_r", [P, P], f32r)
        mask_r = sb("mask_r", [P, P], f32r)
        select_r = sb("select_r", [CS_ROWS, SH], f32r)
        small = sb("small", [P, 2, SH])
        conv_rows = sb("conv_rows", [(TAPS + 1) * CT, P])
        conv_p = sb("conv_p", [P, TAPS + 1, CT])
        wdt = sb("wdt", [P, KD, SH])
        wdt_parts = sb("wdt_parts", [P, KD, CS_ROWS], f32r)
        sumsq = sb("sumsq", [P, 2, 10])
        mean_sq = sb("mean_sq", [P, 10])
        rstd = sb("rstd", [P, 10])
        minus_half = sb("minus_half", [P, 1])
        gu = sb("gu", [P, SEQ])
        gu_hi = sb("gu_hi", [P, 2, SEQ], f32r)
        gu_lo = sb("gu_lo", [P, 2, SEQ], f32r)
        bias_col = sb("bias_col", [CS_ROWS, 1])
        dtT = sb("dtT", [CS_ROWS, SEQ])
        conv_acc = sb("conv_acc", [P, 4, SEQ])
        silu_g = conv_acc[:, 0, :]
        xbc = sb("xbc", [P, CT, SEQ])
        x_tok = sb("x_tok", [P, TT, D_SSM])
        z_silu = sb("z_silu", [P, TT, D_SSM])
        dts = sb("dts", [P, 8, TT, SH])
        cs_rows = sb("cs_rows", [P, TT, CS_ROWS])
        csT = sb("csT", [CS_ROWS, 384], f32r)
        cb = sb("cb", [P, GROUPS, 384])
        decay = sb("decay", [P, 2, 384])
        mix_m = sb("mix_m", [P, 2, 384])
        q_tok = sb("q_tok", [P, TT, D_ATTN])
        k_tok = sb("k_tok", [P, TT, D_ATTN])
        v_tok = sb("v_tok", [P, TT, D_ATTN])
        rot_t = sb("rot_t", [P, TT, HEADS, ROT])
        qT = sb("qT", [P, HEADS // 2, SEQ])
        kT = sb("kT", [P, HEADS // 2, SEQ])
        probs = decay
        probsT = xbc[:, :, :].rearrange("p c l -> p (c l)").rearrange("p (h l) -> p h l", h=HEADS)
        row_max = sb("row_max", [P, HEADS, TT])
        row_bias = sb("row_bias", [P, HEADS, TT])
        row_sum = sb("row_sum", [P, TT, HEADS])
        row_inv = sb("row_inv", [P, TT, HEADS])

        bank = ctx.enter_context(nc.psum_tensor("bank", [P, 8, 512], f32))
        G_BANK, U_BANK = 4, 5
        PAIR_T_BANK = 6
        T_BANKS = (6, 7)

        ident, tri = cst[:, C_ID:C_ID + P], cst[:, C_TRI:C_TRI + SEQ]
        cos_t = cst[:, C_COS:C_COS + TT * ROT].rearrange("p (t r) -> p t r", t=TT)
        sin_t = cst[:, C_SIN:C_SIN + TT * ROT].rearrange("p (t r) -> p t r", t=TT)
        skip16, alog16 = (small[:, j, :] for j in range(2))

        x_loaded = [sem(f"x_loaded{j}") for j in range(2 * TT)]
        ident_loaded = sem("ident_loaded")
        first_loaded = [sem(f"first_loaded{k}") for k in range(3)]
        consts_loaded = sem("consts_loaded")
        params_loaded = sem("params_loaded")
        mix_w_loaded = sem("mix_w_loaded")
        norm_loaded = [sem(f"norm_loaded{n}") for n in range(4)]
        raw_loaded = [sem(f"raw_loaded{s}") for s in range(RAW_SLOTS)]
        hi_ready = sem("hi_ready")
        half_ready = sem("half_ready")
        half_used = sem("half_used")
        consts_r = sem("consts_r")
        wdt_hi_ready = sem("wdt_hi_ready")
        wdt_ready = sem("wdt_ready")
        x_ready = sem("x_ready")
        sq_ready = sem("sq_ready")
        rstd_ready = sem("rstd_ready")
        pool_step = sem("pool_step")
        weighed = sem("weighed")
        scaled_left = sem("scaled_left")
        scaled_right = sem("scaled_right")
        scaled = sem("scaled")
        transposed = sem("transposed")
        hT_hi_ready = sem("hT_hi_ready")
        hT_ready = sem("hT_ready")
        gate_done = sem("gate_done")
        up_done = sem("up_done")
        down_done = sem("down_done")
        silu_ready = sem("silu_ready")
        gu_ready = sem("gu_ready")
        gu_hi_ready = sem("gu_hi_ready")
        gu_split = sem("gu_split")
        pair_used = sem("pair_used")
        pair_done = sem("pair_done")
        pair_silu_ready = sem("pair_silu_ready")
        pair_gu_ready = sem("pair_gu_ready")
        pair_T = sem("pair_T")
        pair_hi_ready = sem("pair_hi_ready")
        acc_ready = sem("acc_ready")
        dve_step = sem("dve_step")
        neg_a_ready = sem("neg_a_ready")
        conv_rows_T = sem("conv_rows_T")
        conv_p_ready = sem("conv_p_ready")
        dtT_done = sem("dtT_done")
        dtT_ready = sem("dtT_ready")
        dt_done = sem("dt_done")
        z0_first = sem("z0_first")
        dt_arg = sem("dt_arg")
        dt_exp = sem("dt_exp")
        atanh_arg = sem("atanh_arg")
        a_ready = sem("a_ready")
        cs_done = sem("cs_done")
        cs_tok_ready = sem("cs_tok_ready")
        csT_done = sem("csT_done")
        csT_ready = sem("csT_ready")
        tap_ready = sem("tap_ready")
        taps_done = sem("taps_done")
        xbc_ready = sem("xbc_ready")
        cb_done = sem("cb_done")
        cb_ready = sem("cb_ready")
        xT_done = sem("xT_done")
        x_tok_ready = sem("x_tok_ready")
        skip_ready = sem("skip_ready")
        proj_out = sem("proj_out")
        bc_done = sem("bc_done")
        decay_ready = sem("decay_ready")
        m_ready = sem("m_ready")
        y_done = sem("y_done")
        y_added = sem("y_added")
        gated = sem("gated")
        rotated = sem("rotated")
        qkT_done = sem("qkT_done")
        qkT_ready = sem("qkT_ready")
        scores_done = sem("scores_done")
        max_ready = sem("max_ready")
        probs_ready = sem("probs_ready")
        probsT_done = sem("probsT_done")
        probsT_ready = sem("probsT_ready")
        pv_done = sem("pv_done")
        out_stored = sem("out_stored")

        block = ctx.enter_context(nc.Block())

        def cols_half(t, half):
            return t.rearrange("p (k f) -> p k f", k=KD)[:, :, half * P:(half + 1) * P]

        def by_tile(t):
            return t.rearrange("p (k f) -> p k f", k=KD)

        def ffn_half(n, i, odd, kind):
            slot = 4 + odd if kind == 2 else 2 * odd + kind
            r = raw[:, (FFN_UNIT0[n] + kind) % RAW_SLOTS, :]
            src = cols_half(r, odd) if kind < 2 else r[:, odd * HALF:(odd + 1) * HALF]
            first = isinstance(i, int) and i < 2
            number = 6 * i + (FFN_HALF0[n] + (slot if first else 3 * odd + kind))
            return number, (FFN_HALF0[n] + slot) % HALF_SLOTS, src

        def mix_half(m):
            r = raw[:, (MIX_UNIT0 + m // 2) % RAW_SLOTS, :]
            src = cols_half(r, m % 2) if by_columns(m) else r[:, (m % 2) * HALF:(m % 2 + 1) * HALF]
            return MIX_HALF0 + m, (MIX_HALF0 + m) % HALF_SLOTS, src

        def ffn_load(eng, n, i, kind):
            s = (FFN_UNIT0[n] + kind) % RAW_SLOTS
            dst = raw[:, s, :]
            if kind < 2:
                src = (w1s, w3s)[kind][n].rearrange("(k p) f -> p k f", p=P)[:, :, bass.ts(i, 2 * P)]
                dst = dst.rearrange("p (k f) -> p k f", k=KD)
            else:
                src = w2s[n].rearrange("(t p) d -> p t d", p=P)[:, bass.ts(i, 2), :]
                dst = dst.rearrange("p (t d) -> p t d", t=2)
            eng.dma_start(dst, src).then_inc(raw_loaded[s], 16)

        def mix_load(eng, u):
            s = (MIX_UNIT0 + u) % RAW_SLOTS
            dst = raw[:, s, :]
            if by_columns(2 * u):
                c = 3 * D_ATTN + D_SSM + CONV_ORDER[2 * u - M_CONV] * P
                src = w_in.rearrange("(k p) f -> p k f", p=P)[:, :, c:c + 2 * P]
                dst = dst.rearrange("p (k f) -> p k f", k=KD)
            elif u < M_OUT // 2:
                c, kk = CHUNK_COL[chunk_of(2 * u)], 4 * (u % 2)
                src = w_in.rearrange("(k p) f -> p k f", p=P)[:, kk:kk + 4, c:c + 512]
                dst = dst.rearrange("p (k f) -> p k f", k=4)
            else:
                r = OUT_ROWS[2 * (u - M_OUT // 2)]
                src = w_out.rearrange("(t p) d -> p t d", p=P)[:, r:r + 2, :]
                dst = dst.rearrange("p (t d) -> p t d", t=2)
            eng.dma_start(dst, src).then_inc(raw_loaded[s], 16)

        @block.sync
        def _(sp):
            def load_x(t, c):
                cols = slice(c * 512, (c + 1) * 512)
                sp.dma_start(x[:, t, cols], x_in[t * P:(t + 1) * P, cols]).then_inc(x_loaded[2 * t + c], 16)

            load_x(0, 0)
            load_x(0, 1)
            sp.dma_start(cst[:, C_ID:C_ID + P], consts[:, C_ID:C_ID + P]).then_inc(ident_loaded, 16)
            sp.dma_start(norm_w[:, 0, :], norms[0].partition_broadcast(P)).then_inc(norm_loaded[0], 16)
            for odd, kind in PAIR_ORDER:
                if (odd, kind) == (1, 0):
                    load_x(1, 0)
                    load_x(1, 1)
                if kind < 2:
                    src = (w1s, w3s)[kind][0].rearrange("(k p) f -> p k f", p=P)[:, :, odd * P:(odd + 1) * P]
                else:
                    src = w2s[0][odd * P:(odd + 1) * P, :]
                sp.dma_start(ffn_half(0, 0, odd, kind)[2], src).then_inc(
                    raw_loaded[kind] if odd else first_loaded[kind], 16)
            sp.dma_start(cst[:, P:], consts[:, P:]).then_inc(consts_loaded, 16)
            for n in range(2):
                for kind in range(3 * n):
                    if n == 1:
                        u = MIX_UNITS - 3 + kind
                        sp.wait_ge(half_ready, MIX_HALF0 + 2 * u + 2)
                    ffn_load(sp, n, 0, kind)
                for kind in range(3):
                    sp.wait_ge(half_ready, ffn_half(n, 0, 1, kind)[0] + 1)
                    ffn_load(sp, n, 1, kind)
                with sp.Fori(2, FI) as i:
                    for kind in range(3):
                        sp.wait_ge(half_ready, i * 6 + (FFN_HALF0[n] - 6 + 3 + kind + 1))
                        ffn_load(sp, n, i, kind)
                if n == 0:
                    for u in range(MIX_UNITS):
                        sp.wait_ge(half_ready, MIX_HALF0 - 3 + u + 1 if u < 3 else MIX_HALF0 + 2 * (u - 3) + 2)
                        mix_load(sp, u)
            for t in range(TT):
                for c in range(2):
                    sp.wait_ge(scaled_right if c else scaled_left, 6 + t + 1)
                    cols = slice(c * 512, (c + 1) * 512)
                    sp.dma_start(out[t * P:(t + 1) * P, cols], normed[:, t, cols]).then_inc(out_stored, 16)
            sp.wait_ge(out_stored, 16 * 2 * TT)

        @block.gpsimd
        def _(pool):
            steps = [0]

            def step(ins):
                steps[0] += 1
                ins.then_inc(pool_step, 1)
                pool.wait_ge(pool_step, steps[0])

            step(pool.memset(minus_half[:, :], -0.5))
            step(pool.memset(cs_rows[:, :, :], 0.0))
            step(pool.memset(bias_col[:, :], 0.0))

            def rsqrt(order, col, width):
                pool.wait_ge(sq_ready, order)
                m = mean_sq[:, col:col + 1]
                if width == D:
                    step(pool.tensor_scalar(m, sumsq[:, 0, col:col + 1], sumsq[:, 1, col:col + 1], EPS, ALU.add, ALU.add))
                else:
                    step(pool.tensor_scalar(m, sumsq[:, 0, col:col + 1], 1.0 / width, EPS, ALU.mult, ALU.add))
                pool.tensor_tensor(rstd[:, col:col + 1], m, minus_half[:, :], ALU.pow).then_inc(rstd_ready, 1)

            def rotate(tok):
                v = tok[:, :, :].rearrange("p t (h d) -> p t h d", h=HEADS)
                for t in range(TT):
                    r = v[:, t, :, 0:ROT]
                    sn = sin_t[:, t, :].unsqueeze(1).to_broadcast([P, HEADS, ROT])
                    cs = cos_t[:, t, :].unsqueeze(1).to_broadcast([P, HEADS, ROT])
                    hr = ROT // 2
                    pool.tensor_tensor(rot_t[:, t, :, 0:hr], r[:, :, hr:ROT], sn[:, :, 0:hr], ALU.mult)
                    step(pool.tensor_tensor(rot_t[:, t, :, hr:ROT], r[:, :, 0:hr], sn[:, :, hr:ROT], ALU.mult))
                    step(pool.tensor_tensor(r, r, cs, ALU.mult))
                    pool.tensor_tensor(r, r, rot_t[:, t, :, :], ALU.add).then_inc(rotated, 1)

            def softplus():
                v, e, w, p, dt = (dts[:, j, :, :] for j in (0, 2, 4, 5, 6))
                pool.wait_ge(atanh_arg, 1)
                step(pool.tensor_tensor(w, e, e, ALU.mult))
                step(pool.tensor_scalar(p, w, 1.0 / 15, None, ALU.mult))
                for k in (13, 11, 9, 7, 5, 3):
                    step(pool.tensor_scalar(p, p, 1.0 / k, None, ALU.add))
                    step(pool.tensor_tensor(p, p, w, ALU.mult))
                step(pool.tensor_scalar(p, p, 1.0, 2.0, ALU.add, ALU.mult))
                step(pool.tensor_tensor(p, p, e, ALU.mult))
                step(pool.tensor_scalar(v, v, 0.0, None, ALU.max))
                step(pool.tensor_tensor(dt, p, v, ALU.add))
                pool.wait_ge(neg_a_ready, 1)
                step(pool.tensor_scalar(w, dt, -1.0, None, ALU.mult))
                pool.tensor_tensor(w, w, dts[:, 3, 0, :].unsqueeze(1).to_broadcast([P, TT, SH]),
                                   ALU.mult).then_inc(a_ready, 1)

            for t in range(TT):
                rsqrt(2 * t + 2, t, D)
            pool.wait_ge(down_done, 6)
            pool.dma_start(wdt[:, :, :], w_in[:, D_IN - SH:D_IN].rearrange("(k p) f -> p k f", p=P)).then_inc(params_loaded, 16)
            pool.dma_start(conv_rows[0:TAPS * CT, :], conv_w.rearrange("k (c p) -> (k c) p", p=P)).then_inc(params_loaded, 16)
            pool.dma_start(conv_rows[TAPS * CT:, :], conv_b.rearrange("(c p) -> c p", p=P)).then_inc(params_loaded, 16)
            for j, v in enumerate((D_skip, A_log)):
                pool.dma_start(small[:, j, :], v.partition_broadcast(P)).then_inc(params_loaded, 16)
            pool.dma_start(bias_col[0:SH, :], dt_bias.rearrange("(h a) -> h a", a=1)).then_inc(params_loaded, 16)
            pool.dma_start(norm_w[:, 1, :], norms[1].partition_broadcast(P)).then_inc(norm_loaded[1], 16)
            pool.dma_start(mix_w[:, 0:D_ATTN], attn_norm.partition_broadcast(P)).then_inc(mix_w_loaded, 16)
            pool.dma_start(mix_w[:, D_ATTN:], ssd_norm.partition_broadcast(P)).then_inc(mix_w_loaded, 16)
            pool.wait_ge(scaled_right, 2)
            pool.dma_start(norm_w[:, 0, :], norms[2].partition_broadcast(P)).then_inc(norm_loaded[2], 16)
            for t in range(TT):
                rsqrt(4 + 2 * t + 2, 2 + t, D)
            pool.wait_ge(weighed, 4)
            pool.dma_start(norm_w[:, 1, :], norms[3].partition_broadcast(P)).then_inc(norm_loaded[3], 16)
            softplus()
            pool.wait_ge(transposed, 8)
            for t in range(TT):
                for j in range(2):
                    pool.wait_ge(x_tok_ready, 2 * j + t + 1)
                    pool.tensor_tensor(
                        normed[:, t, D_ATTN + j * 512:D_ATTN + (j + 1) * 512].rearrange("p (h d) -> p h d", d=SP_),
                        x_tok[:, t, j * 512:(j + 1) * 512].rearrange("p (h d) -> p h d", d=SP_),
                        skip16[:, 8 * j:8 * j + 8].unsqueeze(2).to_broadcast([P, 8, SP_]), ALU.mult).then_inc(skip_ready, 1)
            pool.wait_ge(consts_loaded, 16)
            pool.wait_ge(proj_out, 4)
            rotate(q_tok)
            pool.wait_ge(proj_out, 6)
            rotate(k_tok)
            for t in range(TT):
                rsqrt(8 + t + 1, 4 + t, 512)
            for t in range(TT):
                rsqrt(10 + t + 1, 6 + t, 512)
            for t in range(TT):
                rsqrt(12 + t + 1, 8 + t, 512)
            for n in (2, 3):
                for t in range(TT):
                    rsqrt(14 + 4 * (n - 2) + 2 * t + 2, 2 * (n % 2) + t, D)

        @block.scalar
        def _(act):
            def split_hi(slot, src, loaded, count, columns):
                act.wait_ge(loaded, count)
                dst = w_hi[:, slot, :]
                act.activation(by_tile(dst) if columns else dst, src, ACT.Copy).then_inc(hi_ready, 1)

            def ffn_hi(n, i, odd, kind):
                _, slot, src = ffn_half(n, i, odd, kind)
                u0 = FFN_UNIT0[n] + kind
                split_hi(slot, src, raw_loaded[u0 % RAW_SLOTS], i * 16 + 16 * (u0 // RAW_SLOTS + 1), kind < 2)

            def first_hi(kind):
                _, slot, src = ffn_half(0, 0, 0, kind)
                split_hi(slot, src, first_loaded[kind], 16, kind < 2)

            def mix_hi(m):
                if HALF_SLOTS <= m < MIX_HALVES:
                    act.wait_ge(half_used, m - HALF_SLOTS + 1)
                _, slot, src = mix_half(m)
                u = MIX_UNIT0 + m // 2
                split_hi(slot, src, raw_loaded[u % RAW_SLOTS], 16 * (u // RAW_SLOTS + 1), by_columns(m))

            def square_x(n, t, c):
                if n:
                    act.wait_ge(x_ready, 4 * (n - 1) + 2 * t + c + 1)
                cols, r = slice(c * 512, (c + 1) * 512), 2 * (n % 2) + t
                act.activation(z_silu[:, t, cols], x[:, t, cols], ACT.Square, scale=D ** -0.5,
                               accum_out=sumsq[:, c, r:r + 1]).then_inc(sq_ready, 1)

            def scale_right(n, t):
                act.wait_ge(weighed, 4 * (n - 1) + 2 * t + 2)
                act.wait_ge(rstd_ready, rstd_count(n) + t + 1)
                r, right = 2 * (n % 2) + t, normed[:, t, 512:1024]
                act.activation(right, right, ACT.Identity, scale=rstd[:, r:r + 1]).then_inc(scaled_right, 1)

            def hT_hi_part(count, bank_n, row, t):
                act.wait_ge(transposed, count)
                act.activation(hT_hi[:, row:row + 4, t * P:(t + 1) * P],
                               bank[:, bank_n, :].rearrange("p (k c) -> p k c", k=4), ACT.Copy).then_inc(hT_hi_ready, 1)

            def norm_hi(n, t):
                for j in range(2):
                    hT_hi_part(hT_count(n) + 2 * t + j + 1, T_BANKS[j], 4 * j, t)

            def gate(n, i, odd, downs=0):
                f = looped(n, i, odd)
                act.wait_ge(gate_done, f + 1)
                act.activation(silu_g, bank[:, G_BANK, 0:SEQ], ACT.Silu).then_inc(silu_ready, 1)
                if downs:
                    act.wait_ge(down_done, downs)
                act.wait_ge(gu_ready, f + 1)
                act.activation(gu_hi[:, odd, :], gu[:, :], ACT.Copy).then_inc(gu_hi_ready, 1)

            def ffn_step(n, i, odd):
                i2, odd2 = (i, 1) if not odd else (i + 1, 0)
                ffn_hi(n, i2, odd2, 0)
                ffn_hi(n, i2, odd2, 1)
                gate(n, i, odd)
                act.wait_ge(down_done, (FT - 1) * n + 2 * i + odd)
                ffn_hi(n, i2, odd2, 2)

            def pair_silu(n, t):
                act.wait_ge(pair_done, 2 * n + t + 1)
                g = bank[:, t, :].rearrange("p (j c) -> p j c", j=2)[:, :, 0:P]
                dst = z_silu[:, t, 0:2 * P].rearrange("p (j c) -> p j c", j=2)
                act.activation(dst, g, ACT.Silu).then_inc(pair_silu_ready, 1)

            def first_pair(n):
                pair_silu(n, 0)
                act.wait_ge(pair_used, n + 1)
                ffn_hi(n, 1, 0, 0)
                pair_silu(n, 1)
                ffn_hi(n, 1, 0, 1)
                act.wait_ge(pair_T, 2 * n + 2)
                act.activation(gu_hi[:, :, :], bank[:, PAIR_T_BANK, :].rearrange("p (j l) -> p j l", j=2),
                               ACT.Copy).then_inc(pair_hi_ready, 1)
                ffn_hi(n, 1, 1, 0)
                ffn_hi(n, 1, 1, 1)
                gate(n, 1, 0, (FT - 1) * n + 1)
                for odd in range(2):
                    act.wait_ge(down_done, (FT - 1) * n + odd + 1)
                    ffn_hi(n, 1, odd, 2)

            def ffn_steps(n):
                first_pair(n)
                ffn_step(n, 1, 1)
                with act.Fori(2, FI - 1) as i:
                    ffn_step(n, i, 0)
                    ffn_step(n, i, 1)
                ffn_step(n, FI - 1, 0)

            for c in range(2):
                act.wait_ge(x_loaded[c], 16)
                square_x(0, 0, c)
            first_hi(0)
            norm_hi(0, 0)
            first_hi(1)
            for c in range(2):
                act.wait_ge(x_loaded[2 + c], 16)
                square_x(0, 1, c)
            ffn_hi(0, 0, 1, 0)
            ffn_hi(0, 0, 1, 1)
            norm_hi(0, 1)
            first_hi(2)
            ffn_hi(0, 0, 1, 2)

            ffn_steps(0)
            act.wait_ge(params_loaded, 16 * 6)
            act.activation(wdt_parts[:, :, 0:SH], wdt[:, :, :], ACT.Copy).then_inc(wdt_hi_ready, 1)
            act.activation(wdt_parts[:, :, SH:2 * SH], wdt[:, :, :], ACT.Copy).then_inc(wdt_hi_ready, 1)
            act.wait_ge(consts_loaded, 16)
            act.activation(ident_r[:, :], ident, ACT.Copy).then_inc(consts_r, 1)
            act.activation(mask_r[:, :], cst[:, C_MASK:C_MASK + P], ACT.Copy).then_inc(consts_r, 1)
            act.activation(select_r[:, :], cst[0:CS_ROWS, C_SEL:C_SEL + SH], ACT.Copy).then_inc(consts_r, 1)
            act.wait_ge(conv_rows_T, 1)
            act.activation(conv_p[:, :, :], bank[:, 7, 0:(TAPS + 1) * CT].rearrange("p (k c) -> p k c", c=CT),
                           ACT.Copy).then_inc(conv_p_ready, 1)
            mix_hi(0)
            mix_hi(1)
            gate(0, FI - 1, 1)
            square_x(1, 0, 0)
            square_x(1, 0, 1)
            scale_right(1, 0)
            square_x(1, 1, 0)
            norm_hi(1, 0)
            square_x(1, 1, 1)
            mix_hi(2)
            scale_right(1, 1)
            mix_hi(3)
            norm_hi(1, 1)
            mix_hi(4)
            mix_hi(5)

            def chunk_out(c, t, func, dst):
                if c == "z0" and t == 0:
                    act.wait_ge(z0_first, 1)
                else:
                    act.wait_ge(half_used, M_CHUNK[c] + 4)
                act.activation(dst[:, t, :], bank[:, chunk_bank(c) + t, :], func).then_inc(proj_out, 1)

            def first_tap(j):
                act.wait_ge(half_used, M_CONV + j + 1)
                if j == 0:
                    act.wait_ge(conv_p_ready, 1)
                if j >= 4:
                    act.wait_ge(xbc_ready, j - 3)
                c = CONV_ORDER[j]
                act.activation(conv_acc[:, j % 4, :], bank[:, conv_bank(j), 0:SEQ], ACT.Identity,
                               bias=conv_p[:, TAPS, c:c + 1], scale=conv_p[:, TAPS - 1, c:c + 1]).then_inc(tap_ready, 1)

            def conv_silu(j):
                act.wait_ge(taps_done, j + 1)
                act.activation(xbc[:, CONV_ORDER[j], :], conv_acc[:, j % 4, :], ACT.Silu).then_inc(xbc_ready, 1)

            def x_tok_out(j):
                for t in range(TT):
                    act.wait_ge(xT_done, TT * j + t + 1)
                    act.activation(x_tok[:, t, j * 512:(j + 1) * 512], bank[:, 6 + t, :], ACT.Copy).then_inc(x_tok_ready, 1)

            def decay_exp(h):
                act.wait_ge(bc_done, h + 1)
                if h >= 2:
                    act.wait_ge(m_ready, 2 * (h - 1))
                for s, (a, b) in enumerate(((0, 256), (256, 384))):
                    act.activation(decay[:, h % 2, a:b], bank[:, 4 + h % 2, a:b], ACT.Exp,
                                   bias=dts[:, 7, s, h:h + 1]).then_inc(decay_ready, 1)

            def square_mix(col, first_col, count):
                for t in range(TT):
                    act.wait_ge(gated, count + t + 1)
                    act.activation(conv_acc[:, 2 * t:2 * t + 2, :],
                                   normed[:, t, first_col:first_col + 512].rearrange("p (a b) -> p a b", a=2), ACT.Square,
                                   accum_out=sumsq[:, 0, col + t:col + t + 1]).then_inc(sq_ready, 1)

            def qkT_out(dst, bank0, count):
                for t in range(TT):
                    act.wait_ge(qkT_done, count + t + 1)
                    act.activation(dst[:, :, t * P:(t + 1) * P], bank[:, bank0 + t, :].rearrange("p (k c) -> p k c", k=4),
                                   ACT.Copy).then_inc(qkT_ready, 1)

            def softmax_exp(h):
                act.wait_ge(max_ready, h + 1)
                if h >= 2:
                    act.wait_ge(probsT_done, h - 1)
                for t, (a, b) in enumerate(((0, 128), (128, 384))):
                    act.activation(probs[:, h % 2, a:b], bank[:, score_bank(h), a:b], ACT.Exp,
                                   bias=row_bias[:, h, t:t + 1], scale=HD ** -0.5,
                                   accum_out=row_sum[:, t, h:h + 1]).then_inc(probs_ready, 1)

            def probsT_out(h):
                act.wait_ge(probsT_done, h + 1)
                act.activation(probsT[:, h, :], bank[:, score_bank(h) + 1, 0:384], ACT.Copy).then_inc(probsT_ready, 1)

            for t in range(TT):
                chunk_out("z0", t, ACT.Silu, z_silu[:, :, 0:512])
                if t == 0:
                    for m in (6, 7, 8):
                        mix_hi(m)
            act.wait_ge(dtT_done, 1)
            act.activation(dtT[:, :], bank[0:CS_ROWS, 7, 0:SEQ], ACT.Identity, bias=bias_col[:, :]).then_inc(dtT_ready, 1)
            for m in range(5, MIX_HALVES):
                if m < 17:
                    first_tap(m - 5)
                if m == 32:
                    for t in range(TT):
                        chunk_out("v", t, ACT.Copy, v_tok)
                if 30 <= m < 33:
                    probsT_out(2 * (m - 30))
                    probsT_out(2 * (m - 30) + 1)
                if m in (33, 34):
                    probsT_out(m - 27)
                if 29 <= m < 32:
                    softmax_exp(2 * (m - 29))
                    softmax_exp(2 * (m - 29) + 1)
                if m in (32, 33):
                    softmax_exp(m - 26)
                for split in splits(m):
                    mix_hi(split)
                if m == 6:
                    act.wait_ge(dt_arg, 1)
                    act.activation(dts[:, 2, :, :], dts[:, 1, :, :], ACT.Exp).then_inc(dt_exp, 1)
                    act.activation(dts[:, 3, 0, :], alog16, ACT.Exp).then_inc(neg_a_ready, 1)
                if 7 <= m < 19:
                    conv_silu(m - 7)
                if m == 13:
                    for g in range(GROUPS):
                        act.wait_ge(cb_done, g + 1)
                        act.activation(cb[:, g, :], bank[:, 4 + g, 0:384], ACT.Copy).then_inc(cb_ready, 1)
                if m == 17:
                    x_tok_out(0)
                if m == 19:
                    x_tok_out(1)
                if 20 <= m < 28:
                    decay_exp(2 * (m - 20))
                    decay_exp(2 * (m - 20) + 1)
                if m == 20:
                    for t in range(TT):
                        chunk_out("q", t, ACT.Copy, q_tok)
                if m == 24:
                    for t in range(TT):
                        chunk_out("k", t, ACT.Copy, k_tok)
                if m == 23:
                    qkT_out(qT, 2, 0)
                if m == 25:
                    square_mix(4, D_ATTN, 0)
                if m == 27:
                    qkT_out(kT, 0, TT)
                if m == 28:
                    for t in range(TT):
                        hT_hi_part(8 + t + 1, 4 + t, 8, t)
                    for t in range(TT):
                        chunk_out("z1", t, ACT.Silu, z_silu[:, :, 512:1024])
                if m == 30:
                    square_mix(6, D_ATTN + 512, 2)
                if m == 35:
                    for t in range(TT):
                        hT_hi_part(10 + t + 1, 4 + t, 0, t)
                if m == 36:
                    square_mix(8, 0, 4)
                if m == 39:
                    for t in range(TT):
                        hT_hi_part(12 + t + 1, 4 + t, 4, t)
                if m == 40:
                    for kind in range(2):
                        act.wait_ge(half_used, 39 + kind)
                        ffn_hi(1, 0, 0, kind)
            square_x(2, 0, 0)
            square_x(2, 0, 1)
            scale_right(2, 0)
            norm_hi(2, 0)
            for kind in range(2):
                act.wait_ge(half_used, 41 + kind)
                ffn_hi(1, 0, 1, kind)
            square_x(2, 1, 0)
            square_x(2, 1, 1)
            scale_right(2, 1)
            norm_hi(2, 1)
            for odd in range(2):
                ffn_hi(1, 0, odd, 2)

            ffn_steps(1)
            gate(1, FI - 1, 1)
            for c in range(2):
                square_x(3, 0, c)
            square_x(3, 1, 0)
            square_x(3, 1, 1)
            scale_right(3, 0)
            scale_right(3, 1)

        @block.vector
        def _(dve):
            steps = [0]

            def step(ins):
                steps[0] += 1
                ins.then_inc(dve_step, 1)
                dve.wait_ge(dve_step, steps[0])

            def split_lo(half, columns):
                h, slot, src = half
                dve.wait_ge(hi_ready, h + 1)
                hi, lo = w_hi[:, slot, :].bitcast(f32), w_lo[:, slot, :]
                if columns:
                    hi, lo = by_tile(hi), by_tile(lo)
                dve.tensor_tensor(lo, src, hi, ALU.subtract).then_inc(half_ready, 1)

            def ffn_lo(n, i, odd, kind):
                split_lo(ffn_half(n, i, odd, kind), kind < 2)

            def mix_lo(m):
                split_lo(mix_half(m), by_columns(m))

            def update_x(n, t, c):
                dve.wait_ge(acc_ready, 4 * (n - 1) + 2 * t + c + 1)
                xs = x[:, t, c * 512:(c + 1) * 512]
                dve.scalar_tensor_tensor(xs, bank[:, 2 * t + c, :], 1.0 if n == 2 else 0.5, xs,
                                         ALU.mult, ALU.add).then_inc(x_ready, 1)

            def scale_first(t):
                if t == 0:
                    dve.wait_ge(norm_loaded[0], 16)
                dve.wait_ge(rstd_ready, t + 1)
                for c, done in enumerate((scaled_left, scaled_right)):
                    cols = slice(c * 512, (c + 1) * 512)
                    dve.scalar_tensor_tensor(normed[:, t, cols], x[:, t, cols], rstd[:, t:t + 1], norm_w[:, 0, cols],
                                             ALU.mult, ALU.mult).then_inc(done, 1)

            def weigh_x(n, t, c):
                if t + c == 0:
                    dve.wait_ge(norm_loaded[n], 16)
                dve.wait_ge(x_ready, 4 * (n - 1) + 2 * t + c + 1)
                cols = slice(c * 512, (c + 1) * 512)
                dve.tensor_tensor(normed[:, t, cols], x[:, t, cols], norm_w[:, n % 2, cols], ALU.mult).then_inc(weighed, 1)

            def scale_left(n, t):
                dve.wait_ge(weighed, 4 * (n - 1) + 2 * t + 1)
                dve.wait_ge(rstd_ready, rstd_count(n) + t + 1)
                r, left = 2 * (n % 2) + t, normed[:, t, 0:512]
                dve.tensor_scalar(left, left, rstd[:, r:r + 1], None, ALU.mult).then_inc(scaled_left, 1)

            def hT_lo_part(count, bank_n, row, t):
                dve.wait_ge(hT_hi_ready, count)
                part = slice(t * P, (t + 1) * P)
                dve.tensor_tensor(hT_lo[:, row:row + 4, part],
                                  bank[:, bank_n, :].rearrange("p (k c) -> p k c", k=4),
                                  hT_hi[:, row:row + 4, part].bitcast(f32), ALU.subtract).then_inc(hT_ready, 1)

            def norm_lo(n, t):
                for j in range(2):
                    hT_lo_part(hT_count(n) + 2 * t + j + 1, T_BANKS[j], 4 * j, t)

            def up(n, i, odd):
                f = looped(n, i, odd)
                dve.wait_ge(up_done, f + 1)
                dve.wait_ge(silu_ready, f + 1)
                dve.wait_ge(gu_split, FT * n + 2 * i + odd)
                dve.tensor_tensor(gu[:, :], bank[:, U_BANK, 0:SEQ], silu_g, ALU.mult).then_inc(gu_ready, 1)
                dve.wait_ge(gu_hi_ready, f + 1)
                dve.tensor_tensor(gu_lo[:, odd, :], gu[:, :], gu_hi[:, odd, :].bitcast(f32),
                                  ALU.subtract).then_inc(gu_split, 1)

            def ffn_step(n, i, odd):
                i2, odd2 = (i, 1) if not odd else (i + 1, 0)
                ffn_lo(n, i2, odd2, 0)
                ffn_lo(n, i2, odd2, 1)
                up(n, i, odd)
                ffn_lo(n, i2, odd2, 2)

            def pair_mul(n, t):
                dve.wait_ge(pair_silu_ready, 2 * n + t + 1)
                gu_tok, s = (v[:, t, 0:2 * P].rearrange("p (j c) -> p j c", j=2) for v in (normed, z_silu))
                u = bank[:, t, :].rearrange("p (j c) -> p j c", j=2)[:, :, P:2 * P]
                dve.tensor_tensor(gu_tok, u, s, ALU.mult).then_inc(pair_gu_ready, 1)

            def first_pair(n):
                pair_mul(n, 0)
                ffn_lo(n, 1, 0, 0)
                pair_mul(n, 1)
                ffn_lo(n, 1, 0, 1)
                dve.wait_ge(pair_hi_ready, n + 1)
                dve.tensor_tensor(gu_lo[:, :, :], bank[:, PAIR_T_BANK, :].rearrange("p (j l) -> p j l", j=2),
                                  gu_hi[:, :, :].bitcast(f32), ALU.subtract).then_inc(gu_split, 2)
                ffn_lo(n, 1, 1, 0)
                ffn_lo(n, 1, 1, 1)
                up(n, 1, 0)
                ffn_lo(n, 1, 0, 2)
                ffn_lo(n, 1, 1, 2)

            def ffn_steps(n):
                first_pair(n)
                ffn_step(n, 1, 1)
                with dve.Fori(2, FI - 1) as i:
                    ffn_step(n, i, 0)
                    ffn_step(n, i, 1)
                ffn_step(n, FI - 1, 0)

            for c in range(2):
                dve.wait_ge(x_loaded[c], 16)
            scale_first(0)
            ffn_lo(0, 0, 0, 0)
            norm_lo(0, 0)
            for c in range(2):
                dve.wait_ge(x_loaded[2 + c], 16)
            ffn_lo(0, 0, 0, 1)
            scale_first(1)
            ffn_lo(0, 0, 1, 0)
            ffn_lo(0, 0, 1, 1)
            norm_lo(0, 1)
            ffn_lo(0, 0, 0, 2)
            ffn_lo(0, 0, 1, 2)

            ffn_steps(0)
            dve.wait_ge(wdt_hi_ready, 2)
            dve.tensor_tensor(wdt_parts[:, :, 2 * SH:], wdt[:, :, :], wdt_parts[:, :, 0:SH].bitcast(f32),
                              ALU.subtract).then_inc(wdt_ready, 1)
            mix_lo(0)
            mix_lo(1)
            up(0, FI - 1, 1)
            update_x(1, 0, 0)
            update_x(1, 0, 1)
            weigh_x(1, 0, 0)
            weigh_x(1, 0, 1)
            update_x(1, 1, 0)
            scale_left(1, 0)
            update_x(1, 1, 1)
            norm_lo(1, 0)
            weigh_x(1, 1, 0)
            weigh_x(1, 1, 1)
            scale_left(1, 1)
            mix_lo(2)
            mix_lo(3)
            norm_lo(1, 1)
            mix_lo(4)
            mix_lo(5)

            v, ncs = (dts[:, j, :, :] for j in (0, 7))

            def softplus_argument():
                dve.wait_ge(dt_done, 1)
                step(dve.tensor_copy(v, bank[:, 6, 0:TT * SH].rearrange("p (t h) -> p t h", t=TT)))
                dve.scalar_tensor_tensor(dts[:, 1, :, :], v, -1.0, v, ALU.mult, ALU.min).then_inc(dt_arg, 1)

            def atanh_argument():
                e, w, p = (dts[:, j, :, :] for j in (2, 4, 5))
                dve.wait_ge(dt_exp, 1)
                step(dve.tensor_scalar(w, e, 2.0, None, ALU.add))
                step(dve.reciprocal(p, w))
                dve.tensor_tensor(e, e, p, ALU.mult).then_inc(atanh_arg, 1)

            def cumsum_out():
                dve.wait_ge(cs_done, 1)
                cs = bank[:, 6, 0:TT * SH].rearrange("p (t h) -> p t h", t=TT)
                dve.tensor_copy(cs_rows[:, :, 0:SH], cs).then_inc(cs_tok_ready, 1)
                dve.tensor_copy(cs_rows[:, :, 2 * SH:], cs).then_inc(cs_tok_ready, 1)
                dve.wait_ge(cs_tok_ready, 2)
                step(dve.tensor_scalar(ncs, cs_rows[:, :, 0:SH], -1.0, None, ALU.mult))

            def cumsum_T_out():
                dve.wait_ge(csT_done, 1)
                step(dve.tensor_copy(csT[:, :], bank[0:CS_ROWS, 7, 0:384]))
                lo = slice(2 * SH, CS_ROWS)
                dve.tensor_tensor(csT[lo, :], bank[lo, 7, 0:384], csT[lo, :].bitcast(f32),
                                  ALU.subtract).then_inc(csT_ready, 1)

            def conv_taps(j0):
                dve.wait_ge(tap_ready, j0 + 2)
                done = {}
                for s in (1, 2, 3):
                    for j in (j0, j0 + 1):
                        acc, u, c = conv_acc[:, j % 4, :], bank[:, conv_bank(j), :], CONV_ORDER[j]
                        if s > 1:
                            dve.wait_ge(dve_step, done[j])
                        ins = dve.scalar_tensor_tensor(acc[:, s:SEQ], u[:, 0:SEQ - s],
                                                       conv_p[:, TAPS - 1 - s, c:c + 1], acc[:, s:SEQ],
                                                       ALU.mult, ALU.add)
                        if s < 3:
                            steps[0] += 1
                            ins.then_inc(dve_step, 1)
                            done[j] = steps[0]
                        else:
                            ins.then_inc(taps_done, 1)

            def weigh(h):
                g = h // 8
                if h == 0:
                    dve.wait_ge(cb_ready, 2)
                if h >= 2:
                    dve.wait_ge(y_done, h - 1)
                for s, (a, b) in enumerate(((0, 256), (256, 384))):
                    dve.wait_ge(decay_ready, 2 * h + s + 1)
                    dve.scalar_tensor_tensor(mix_m[:, h % 2, a:b], cb[:, g, a:b], dts[:, 6, s, h:h + 1],
                                             decay[:, h % 2, a:b], ALU.mult, ALU.mult).then_inc(m_ready, 1)

            def ssd_add(g):
                cols = slice(D_ATTN + 512 * g, D_ATTN + 512 * (g + 1))
                dve.wait_ge(y_done, 8 * (g + 1))
                dve.wait_ge(skip_ready, 4)
                for t in range(TT):
                    dve.tensor_tensor(normed[:, t, cols], bank[:, 6 + t, :], normed[:, t, cols], ALU.add).then_inc(y_added, 1)

            def ssd_gate(g):
                cols = slice(D_ATTN + 512 * g, D_ATTN + 512 * (g + 1))
                for t in range(TT):
                    dve.wait_ge(y_added, 2 * g + t + 1)
                    dve.wait_ge(proj_out, 8 if g else 2)
                    dve.tensor_tensor(normed[:, t, cols], normed[:, t, cols], z_silu[:, t, 512 * g:512 * (g + 1)],
                                      ALU.mult).then_inc(gated, 1)

            def mix_scale(col, cols, count):
                dve.wait_ge(mix_w_loaded, 32)
                for t in range(TT):
                    dve.wait_ge(rstd_ready, count + t + 1)
                    dve.scalar_tensor_tensor(normed[:, t, cols], normed[:, t, cols], rstd[:, col + t:col + t + 1],
                                             mix_w[:, cols], ALU.mult, ALU.mult).then_inc(scaled, 1)

            def score_max(h):
                dve.wait_ge(scores_done, h + 1)
                dve.reduce_max(row_max[:, h, 0:1], bank[:, score_bank(h), 0:128], axis=AX.X)
                step(dve.reduce_max(row_max[:, h, 1:2], bank[:, score_bank(h), 128:384], axis=AX.X))
                dve.tensor_scalar(row_bias[:, h, :], row_max[:, h, :], -(HD ** -0.5), None, ALU.mult).then_inc(max_ready, 1)

            def attention_out():
                dve.wait_ge(probs_ready, 2 * HEADS)
                step(dve.reciprocal(row_inv[:, :, :], row_sum[:, :, :]))
                dve.wait_ge(pv_done, HEADS)
                for t in range(TT):
                    dve.tensor_tensor(normed[:, t, 0:D_ATTN].rearrange("p (h d) -> p h d", d=HD),
                                      bank[:, 6 + t, :].rearrange("p (h d) -> p h d", d=HD),
                                      row_inv[:, t, :].unsqueeze(2).to_broadcast([P, HEADS, HD]), ALU.mult).then_inc(gated, 1)

            for m in (6, 7, 8):
                mix_lo(m)
            softplus_argument()
            for m in range(5, MIX_HALVES):
                if m in (24, 28):
                    ssd_add(m // 4 - 6)
                if m == 28:
                    for t in range(TT):
                        hT_lo_part(8 + t + 1, 4 + t, 8, t)
                if m == 24:
                    weigh(8)
                    weigh(9)
                if 29 <= m < 32:
                    score_max(2 * (m - 29))
                    score_max(2 * (m - 29) + 1)
                if m in (32, 33):
                    score_max(m - 26)
                for split in splits(m):
                    mix_lo(split)
                if m < 18 and m % 2 == 0:
                    conv_taps(m - 6)
                if m == 7:
                    atanh_argument()
                if m == 13:
                    cumsum_out()
                if m == 15:
                    cumsum_T_out()
                if 20 <= m < 28 and m != 24:
                    weigh(2 * (m - 20))
                    weigh(2 * (m - 20) + 1)
                if m == 24:
                    ssd_gate(0)
                if m == 26:
                    mix_scale(4, slice(D_ATTN, D_ATTN + 512), 4)
                if m == 29:
                    ssd_gate(1)
                if m == 32:
                    mix_scale(6, slice(D_ATTN + 512, D_MIX), 6)
                if m == 35:
                    for t in range(TT):
                        hT_lo_part(10 + t + 1, 4 + t, 0, t)
                    attention_out()
                if m == 37:
                    mix_scale(8, slice(0, D_ATTN), 8)
                if m == 39:
                    for t in range(TT):
                        hT_lo_part(12 + t + 1, 4 + t, 4, t)
                if m == 40:
                    for kind in range(2):
                        ffn_lo(1, 0, 0, kind)
            update_x(2, 0, 0)
            update_x(2, 0, 1)
            weigh_x(2, 0, 0)
            weigh_x(2, 0, 1)
            scale_left(2, 0)
            norm_lo(2, 0)
            update_x(2, 1, 0)
            weigh_x(2, 1, 0)
            update_x(2, 1, 1)
            ffn_lo(1, 0, 1, 0)
            weigh_x(2, 1, 1)
            scale_left(2, 1)
            ffn_lo(1, 0, 1, 1)
            norm_lo(2, 1)
            ffn_lo(1, 0, 0, 2)
            ffn_lo(1, 0, 1, 2)

            ffn_steps(1)
            up(1, FI - 1, 1)
            update_x(3, 0, 0)
            update_x(3, 0, 1)
            weigh_x(3, 0, 0)
            update_x(3, 1, 0)
            weigh_x(3, 0, 1)
            update_x(3, 1, 1)
            scale_left(3, 0)
            weigh_x(3, 1, 0)
            weigh_x(3, 1, 1)
            scale_left(3, 1)

        @block.tensor
        def _(pe):
            def three(dst, lhs, rhs, start, stop):
                pe.matmul(dst, lhs[0], rhs[0], start=start, stop=False, skip_group_check=True)
                pe.matmul(dst, lhs[0], rhs[1], start=False, stop=False, skip_group_check=True)
                return pe.matmul(dst, lhs[1], rhs[0], start=False, stop=stop, skip_group_check=True)

            def hT(k, part):
                return hT_hi[:, k, part], hT_lo[:, k, part]

            def w_cols(slot, k):
                return tuple(w[:, slot, k * P:(k + 1) * P] for w in (w_hi, w_lo))

            def tok(t):
                return slice(t * P, (t + 1) * P)

            def columns_product(slot, dst, part=slice(0, SEQ), tiles=range(KD)):
                for k in tiles:
                    last = three(dst[:, part], w_cols(slot, k), hT(k, part), k == 0, k == KD - 1)
                return last

            def down(n, i, odd, t, c, start, stop):
                slot = ffn_half(n, i, odd, 2)[1]
                return three(bank[:, 2 * t + c, :], (gu_hi[:, odd, tok(t)], gu_lo[:, odd, tok(t)]),
                             tuple(w[:, slot, c * 512:(c + 1) * 512] for w in (w_hi, w_lo)), start, stop)

            def down_both(n, i, odd, start):
                for t in range(TT):
                    for c in range(2):
                        last = down(n, i, odd, t, c, start, False)
                last.then_inc(down_done, 1)

            def down_waits(n, i, odd):
                pe.wait_ge(half_ready, ffn_half(n, i, odd, 2)[0] + 1)
                pe.wait_ge(gu_split, FT * n + 2 * i + odd + 1)

            def gate_or_up(n, i, odd, kind):
                dst, done, free = ((G_BANK, gate_done, silu_ready), (U_BANK, up_done, gu_ready))[kind]
                f, (h, slot, _) = looped(n, i, odd), ffn_half(n, i, odd, kind)
                pe.wait_ge(half_ready, h + 1)
                if not (isinstance(f, int) and f == 0):
                    pe.wait_ge(free, f)
                columns_product(slot, bank[:, dst, :]).then_inc(done, 1)

            def gate_up(n, i, odd):
                gate_or_up(n, i, odd, 0)
                gate_or_up(n, i, odd, 1)

            def pair_product(n, t, odd):
                s = ffn_half(n, 0, odd, 0)[1]
                dst = bank[:, t, odd * 2 * P:(odd + 1) * 2 * P].rearrange("p (w c) -> p w c", w=2)
                for k in range(KD):
                    if odd == 0 and k % 4 == 0:
                        pe.wait_ge(hT_ready, hT_count(2 * n) + 2 * t + k // 4 + 1)
                    last = three(dst, hT(k, tok(t)), tuple(w[:, s:s + 2, k * P:(k + 1) * P] for w in (w_hi, w_lo)),
                                 k == 0, k == KD - 1)
                return last

            def pair_transposes(n, t):
                pe.wait_ge(pair_gu_ready, 2 * n + t + 1)
                for j in range(2):
                    a = j * SEQ + t * P
                    last = pe.transpose(bank[:, PAIR_T_BANK, a:a + P], normed[:, t, j * P:(j + 1) * P], ident)
                last.then_inc(pair_T, 1)

            def keep_clock(count):
                for _ in range(count):
                    pe.matmul(bank[:, U_BANK, 0:P], ident, ident, start=True, stop=True)

            def ffn(n):
                if n == 0:
                    norm_transposes(0, 0)
                    keep_clock(11)
                h0 = FFN_HALF0[n]
                pe.wait_ge(half_ready, h0 + 2)
                pair_product(n, 0, 0)
                norm_transposes(2 * n, 1)
                pe.wait_ge(half_ready, h0 + 4)
                pair_product(n, 0, 1).then_inc(pair_done, 1)
                pair_product(n, 1, 0).then_inc(pair_used, 1)
                pair_product(n, 1, 1).then_inc(pair_done, 1)
                gate_or_up(n, 1, 0, 0)
                for t in range(TT):
                    pair_transposes(n, t)
                gate_or_up(n, 1, 0, 1)
                down_waits(n, 0, 0)
                down_both(n, 0, 0, True)
                down_waits(n, 0, 1)
                down_both(n, 0, 1, False)
                gate_up(n, 1, 1)
                down_waits(n, 1, 0)
                down_both(n, 1, 0, False)
                with pe.Fori(2, FI - 1) as i:
                    gate_up(n, i, 0)
                    down_waits(n, i - 1, 1)
                    down_both(n, i - 1, 1, False)
                    gate_up(n, i, 1)
                    down_waits(n, i, 0)
                    down_both(n, i, 0, False)
                i = FI - 1
                if n == 0:
                    pe.wait_ge(params_loaded, 16 * 6)
                    pe.transpose(bank[:, 7, 0:(TAPS + 1) * CT], conv_rows[:, :],
                                 cst[0:(TAPS + 1) * CT, C_ID:C_ID + (TAPS + 1) * CT]).then_inc(conv_rows_T, 1)
                gate_up(n, i, 0)
                down_waits(n, i - 1, 1)
                down_both(n, i - 1, 1, False)
                gate_up(n, i, 1)
                down_waits(n, i, 0)
                for c in range(2):
                    down(n, i, 0, 0, c, False, False)
                down_waits(n, i, 1)
                for c in range(2):
                    down(n, i, 1, 0, c, False, True).then_inc(acc_ready, 1)
                for c in range(2):
                    last = down(n, i, 0, 1, c, False, False)
                    if c:
                        last.then_inc(down_done, 1)
                    down(n, i, 1, 1, c, False, True).then_inc(acc_ready, 1)

            def transpose_rows(t, col, bank_n):
                for k in range(4):
                    last = pe.transpose(bank[:, bank_n, k * P:(k + 1) * P],
                                        normed[:, t, col + k * P:col + (k + 1) * P], ident)
                last.then_inc(transposed, 1)

            def norm_transposes(n, t):
                for j in range(2):
                    pe.wait_ge(scaled_right if j else scaled_left, 2 * n + t + 1)
                    if t:
                        pe.wait_ge(hT_ready, hT_count(n) + j + 1)
                    transpose_rows(t, 512 * j, T_BANKS[j])

            pe.wait_ge(ident_loaded, 16)
            keep_clock(5)
            ffn(0)

            def dt_product():
                pe.wait_ge(wdt_ready, 1)
                for k in range(KD):
                    h_hi, h_lo = hT(k, slice(0, SEQ))
                    pe.matmul(bank[0:CS_ROWS, 7, 0:SEQ], wdt_parts[:, k, :], h_hi, start=k == 0, stop=False,
                              skip_group_check=True)
                    last = pe.matmul(bank[0:SH, 7, 0:SEQ], wdt_parts[:, k, 0:SH], h_lo, start=False,
                                     stop=k == KD - 1, skip_group_check=True)
                last.then_inc(dtT_done, 1)

            def dt_transposes():
                pe.wait_ge(dtT_ready, 1)
                pe.wait_ge(consts_loaded, 16)
                for t in range(TT):
                    last = pe.matmul(bank[:, 6, t * SH:(t + 1) * SH], dtT[:, tok(t)], cst[0:CS_ROWS, C_SEL:C_SEL + SH],
                                     start=True, stop=True)
                last.then_inc(dt_done, 1)

            def conv_half(j):
                pe.wait_ge(half_ready, MIX_HALF0 + M_CONV + j + 1)
                if j >= 4:
                    pe.wait_ge(taps_done, j - 3)
                if j in (2, 3):
                    pe.wait_ge(proj_out, j - 1)
                columns_product(mix_half(M_CONV + j)[1], bank[:, conv_bank(j), :]).then_inc(half_used, 1)

            def cumsum():
                pe.wait_ge(a_ready, 1)
                a = dts[:, 4, :, :]
                pe.matmul(bank[:, 6, 0:SH], tri[:, 0:P], a[:, 0, :], start=True, stop=True)
                pe.matmul(bank[:, 6, SH:2 * SH], tri[:, P:SEQ], a[:, 0, :], start=True, stop=False)
                pe.matmul(bank[:, 6, SH:2 * SH], tri[:, 0:P], a[:, 1, :], start=False, stop=True).then_inc(cs_done, 1)

            def cumsum_T():
                pe.wait_ge(cs_tok_ready, 2)
                for j, t in enumerate((0, 1, 1)):
                    last = pe.transpose(bank[0:CS_ROWS, 7, j * P:(j + 1) * P], cs_rows[:, t, :], ident)
                last.then_inc(csT_done, 1)

            def cb_products():
                pe.wait_ge(xbc_ready, 4)
                for g in range(GROUPS):
                    b, c = xbc[:, 8 + g, :], xbc[:, 10 + g, :]
                    pe.matmul(bank[:, 4 + g, 0:SEQ], b[:, 0:P], c, start=True, stop=True)
                    pe.matmul(bank[:, 4 + g, SEQ:SEQ + P], b[:, P:SEQ], c[:, P:SEQ], start=True, stop=True).then_inc(cb_done, 1)

            def x_transposes(j):
                pe.wait_ge(xbc_ready, 4 + 4 * (j + 1))
                if j == 1:
                    pe.wait_ge(x_tok_ready, 2)
                else:
                    pe.wait_ge(csT_ready, 1)
                for t in range(TT):
                    for k in range(4):
                        last = pe.transpose(bank[:, 6 + t, k * P:(k + 1) * P], xbc[:, 4 * j + k, tok(t)], ident)
                    last.then_inc(xT_done, 1)

            def chunk_part(m, t):
                b, q, slot = chunk_bank(chunk_of(m)), m % 4, mix_half(m)[1]
                for k in range(2):
                    last = three(bank[:, b + t, :], hT(2 * q + k, tok(t)),
                                 tuple(w[:, slot, k * 512:(k + 1) * 512] for w in (w_hi, w_lo)),
                                 q == 0 and k == 0, q == 3 and k == 1)
                return last

            def first_chunk():
                norm_transposes(1, 0)
                keep_clock(5)
                for t in range(TT):
                    for m in range(4):
                        pe.wait_ge(hT_ready, 4 + 2 * t + m // 2 + 1)
                        if t == 0 and m == 2:
                            norm_transposes(1, 1)
                        if t == 0:
                            pe.wait_ge(half_ready, MIX_HALF0 + m + 1)
                        last = chunk_part(m, t)
                        if t == 1:
                            last.then_inc(half_used, 1)
                        elif m == 3:
                            last.then_inc(z0_first, 1)

            def chunk_half(m):
                pe.wait_ge(half_ready, MIX_HALF0 + m + 1)
                if m == M_CHUNK["q"]:
                    pe.wait_ge(taps_done, 10)
                if m == M_CHUNK["k"]:
                    pe.wait_ge(taps_done, 12)
                if m == M_CHUNK["z1"]:
                    pe.wait_ge(qkT_ready, 2)
                if m == M_CHUNK["v"]:
                    pe.wait_ge(qkT_ready, 4)
                chunk_part(m, 0)
                chunk_part(m, 1).then_inc(half_used, 1)

            def diagonal_blocks(b):
                return b[:, 0:384].rearrange("p (j c) -> p j c", c=P)[:, 0:3:2, :]

            def twice(square):
                return square[:, :].unsqueeze(1).to_broadcast([P, 2, P])

            def decay_args(h):
                b = bank[:, 4 + h % 2, :]
                if h >= 2:
                    pe.wait_ge(decay_ready, 2 * (h - 1))
                else:
                    pe.wait_ge(cb_ready, 2)
                    pe.wait_ge(csT_ready, 1)
                    pe.wait_ge(consts_r, 3)
                pe.matmul(b[:, 0:384], select_r[:, h:h + 1].to_broadcast([CS_ROWS, P]), csT[:, :],
                          start=True, stop=False, skip_group_check=True)
                pe.matmul(diagonal_blocks(b), ident_r[:, :], twice(mask_r), start=False, stop=True,
                          skip_group_check=True).then_inc(bc_done, 1)

            def ssd_out(h):
                pe.wait_ge(m_ready, 2 * (h + 1))
                if h == 0:
                    pe.wait_ge(x_tok_ready, 4)
                if h == 8:
                    pe.wait_ge(y_added, 2)
                m, c, o = mix_m[:, h % 2, :], slice(h * SP_, (h + 1) * SP_), slice((h % 8) * SP_, (h % 8 + 1) * SP_)
                pe.matmul(bank[:, 6, o], m[:, 0:P], x_tok[:, 0, c], start=True, stop=True)
                pe.matmul(bank[:, 7, o], m[:, P:SEQ], x_tok[:, 0, c], start=True, stop=False)
                pe.matmul(bank[:, 7, o], m[:, SEQ:SEQ + P], x_tok[:, 1, c], start=False, stop=True).then_inc(y_done, 1)

            def mix_transposes(count, col, free, free_count):
                pe.wait_ge(free, free_count)
                for t in range(TT):
                    pe.wait_ge(scaled, count + t + 1)
                    transpose_rows(t, col, 4 + t)

            def qk_transposes(tensor, bank0, count):
                pe.wait_ge(rotated, count)
                for t in range(TT):
                    for k in range(4):
                        last = pe.transpose(bank[:, bank0 + t, k * P:(k + 1) * P], tensor[:, t, k * P:(k + 1) * P], ident)
                    last.then_inc(qkT_done, 1)

            def scores(h):
                r, p, b = slice(HD * (h % 2), HD * (h % 2 + 1)), h // 2, bank[:, score_bank(h), :]
                if h == 0:
                    pe.wait_ge(qkT_ready, 4)
                    pe.wait_ge(hT_ready, 10)
                if h == 1:
                    pe.wait_ge(proj_out, 8)
                if h >= 2:
                    pe.wait_ge(probs_ready, 2 * (h - 1) if h < 7 else 2 * h)
                pe.matmul(b[:, 0:P], qT[r, p, 0:P], kT[r, p, 0:P], start=True, stop=False, skip_group_check=True)
                pe.matmul(b[:, P:P + SEQ], qT[r, p, P:SEQ], kT[r, p, :], start=False, stop=False, skip_group_check=True)
                pe.matmul(diagonal_blocks(b), mask_r[:, :], twice(ident_r), start=False, stop=True,
                          skip_group_check=True).then_inc(scores_done, 1)

            def probs_transposes(h):
                pe.wait_ge(probs_ready, 2 * (h + 1))
                if h >= 2:
                    pe.wait_ge(probsT_ready, h - 1 if h < 7 else h)
                for a in range(3):
                    last = pe.transpose(bank[:, score_bank(h) + 1, a * P:(a + 1) * P],
                                        probs[:, h % 2, a * P:(a + 1) * P], ident)
                last.then_inc(probsT_done, 1)

            def pv(h):
                pe.wait_ge(probsT_ready, h + 1)
                if h == 0:
                    pe.wait_ge(proj_out, 10)
                    pe.wait_ge(y_added, 4)
                pt, c = probsT[:, h, :], slice(h * HD, (h + 1) * HD)
                pe.matmul(bank[:, 6, c], pt[:, 0:P], v_tok[:, 0, c], start=True, stop=True)
                pe.matmul(bank[:, 7, c], pt[:, P:SEQ], v_tok[:, 0, c], start=True, stop=False)
                pe.matmul(bank[:, 7, c], pt[:, SEQ:SEQ + P], v_tok[:, 1, c], start=False, stop=True).then_inc(pv_done, 1)

            def out_part(j, t, c):
                slot = mix_half(M_OUT + j)[1]
                return three(bank[:, 2 * t + c, :], hT(mix_row(OUT_ROWS[j]), tok(t)),
                             tuple(w[:, slot, c * 512:(c + 1) * 512] for w in (w_hi, w_lo)), j == 0, j == 11)

            def out_half(j):
                pe.wait_ge(half_ready, MIX_HALF0 + M_OUT + j + 1)
                if j == 0:
                    pe.wait_ge(proj_out, 10)
                    pe.wait_ge(hT_ready, 10)
                if j == 4:
                    pe.wait_ge(hT_ready, 12)
                for t in range(TT):
                    if j == 0 and t == 1:
                        pe.wait_ge(probsT_ready, 6)
                    for c in range(2):
                        last = out_part(j, t, c)
                last.then_inc(half_used, 1)

            def out_attention():
                pe.wait_ge(hT_ready, 14)
                for c in range(2):
                    for j in range(8, 12):
                        if c == 0:
                            pe.wait_ge(half_ready, MIX_HALF0 + M_OUT + j + 1)
                        last = out_part(j, 0, c)
                    last.then_inc(acc_ready, 1)
                for j in (8, 9):
                    out_part(j, 1, 0)
                    out_part(j, 1, 1).then_inc(half_used, 1)
                norm_transposes(2, 0)
                for c in range(2):
                    out_part(10, 1, c)
                    out_part(11, 1, c).then_inc(acc_ready, 1)

            first_chunk()
            dt_product()
            for m in range(M_CONV, M_OUT + 8):
                if m < M_CONV + CT:
                    conv_half(m - M_CONV)
                elif m < M_OUT:
                    chunk_half(m)
                else:
                    out_half(m - M_OUT)
                if m == 4:
                    dt_transposes()
                if m == 12:
                    cumsum()
                    cb_products()
                if m == 14:
                    cumsum_T()
                if m == 16:
                    x_transposes(0)
                if m == 18:
                    x_transposes(1)
                if m == 19:
                    decay_args(0)
                    decay_args(1)
                if 20 <= m < 28:
                    for h in (2 * (m - 20), 2 * (m - 20) + 1):
                        ssd_out(h)
                        if h + 2 < SH:
                            decay_args(h + 2)
                if m == 22:
                    qk_transposes(q_tok, 2, 2)
                if m == 26:
                    qk_transposes(k_tok, 0, 4)
                if m == 27:
                    mix_transposes(0, D_ATTN, decay_ready, 2 * SH)
                if 29 <= m < 32:
                    probs_transposes(2 * (m - 29))
                    probs_transposes(2 * (m - 29) + 1)
                if 28 <= m < 31:
                    scores(2 * (m - 28))
                    scores(2 * (m - 28) + 1)
                if m == 32:
                    probs_transposes(6)
                if m in (31, 32):
                    scores(m - 25)
                if m == 32:
                    for h in range(4):
                        pv(h)
                if m == 33:
                    probs_transposes(7)
                    pv(4)
                    pv(5)
                if m == 34:
                    pv(6)
                    pv(7)
                    mix_transposes(2, D_ATTN + 512, probsT_ready, HEADS)
                if m == 38:
                    mix_transposes(4, 0, hT_ready, 12)
            out_attention()
            ffn(1)


def by_columns(m):
    return M_CONV <= m < M_CONV + CT


def chunk_of(m):
    return next(c for c in CHUNKS if M_CHUNK[c] <= m < M_CHUNK[c] + 4)


def splits(m):
    return [] if m == 31 else [35, 36] if m == 32 else [m + 4] if m + 4 < MIX_HALVES else []


def looped(n, i, odd):
    return (FT - 2) * n + 2 * i + (odd - 2)


def rstd_count(n):
    return (0, 2, 10, 12)[n]


def hT_count(n):
    return (0, 4, 14)[n]


def chunk_bank(c):
    return {"z0": 0, "q": 2, "k": 0, "z1": 2, "v": 0}[c]


def conv_bank(j):
    return (j + 2) % 4


def score_bank(h):
    return 2 if h in (1, 3, 5) else 4


_INS = ["x", "ffn1_norm", "ffn1_w1", "ffn1_w3", "ffn1_w2", "mix_norm", "w_in", "conv_w", "conv_b",
        "dt_bias", "A_log", "D_skip", "attn_out_norm", "ssd_out_norm", "w_out",
        "ffn2_norm", "ffn2_w1", "ffn2_w3", "ffn2_w2", "final_norm"]


def kernel(**inputs):
    import concourse.bacc as bacc
    from concourse.bass_utils import run_bass_kernel_spmd

    nc = bacc.Bacc("TRN2", target_bir_lowering=False, num_devices=1)
    arrays, t = {}, {}
    for name in _INS + ["shape_constants"]:
        if name == "shape_constants":
            a = shape_constants()
        else:
            a = np.ascontiguousarray(inputs[name])
            if name != "final_norm":
                a = a[0]
        arrays[f"in_{name}"] = a
        t[name] = nc.dram_tensor(f"in_{name}", a.shape, mybir.dt.from_np(a.dtype), kind="ExternalInput").ap()
    out = nc.dram_tensor("out_x", (SEQ, D), mybir.dt.float32, kind="ExternalOutput").ap()
    build(nc, t["x"], (t["ffn1_w1"], t["ffn2_w1"]), (t["ffn1_w3"], t["ffn2_w3"]), (t["ffn1_w2"], t["ffn2_w2"]),
          (t["ffn1_norm"], t["mix_norm"], t["ffn2_norm"], t["final_norm"]), t["w_in"], t["conv_w"], t["conv_b"],
          t["dt_bias"], t["A_log"], t["D_skip"], t["attn_out_norm"], t["ssd_out_norm"], t["w_out"],
          t["shape_constants"], out)
    r = run_bass_kernel_spmd(nc, [arrays], core_ids=[0])
    return r.results[0]["out_x"].reshape(1, SEQ, D)
```
